# Optimizing a Trainium2 kernel written in Bass

```python
import jax
import jax.numpy as jnp
from jax import lax
import numpy as np

D_MODEL = 1024
BATCH = 1
SEQ = 256
DEPTH = 2

CTX_LEN = 256
GRID_W = 64
HEAD_DIM = 64
NA_HEADS = 4
NA_ROWS = 8
NA_COLS = 16
GQA_HEADS = 8
GQA_KV_HEADS = 2
MLA_HEADS = 4
MLA_Q_RANK = 256
MLA_KV_RANK = 128
MLA_NOPE = 64
MLA_ROPE = 32
MLA_V = 64
N_BRANCH = 3
N_MOD = 9
D_FF = ((8 * D_MODEL // 3 + 127) // 128) * 128
Q_BLOCK = 128
ROPE_THETA = 10000.0
EPS = 1e-6
NEG_BIG = -1e30

NA_WIDTH = NA_HEADS * HEAD_DIM
GQA_Q_WIDTH = GQA_HEADS * HEAD_DIM
GQA_KV_WIDTH = GQA_KV_HEADS * HEAD_DIM
MLA_OUT_WIDTH = MLA_HEADS * MLA_V
IN_SIZES = (NA_WIDTH, NA_WIDTH, NA_WIDTH, GQA_Q_WIDTH, GQA_KV_WIDTH, GQA_KV_WIDTH,
            MLA_Q_RANK, MLA_KV_RANK, MLA_ROPE, N_BRANCH * D_MODEL)
IN_SPLITS = tuple(int(s) for s in np.cumsum(IN_SIZES)[:-1])
IN_WIDTH = sum(IN_SIZES)

kernel_name = "hybrid_na_gqa_mla_macaron_dit"

def rmsnorm(x, g):
    xf = x.astype(jnp.float32)
    y = xf * lax.rsqrt(jnp.mean(xf * xf, axis=-1, keepdims=True) + EPS)
    return (y * g.astype(jnp.float32)).astype(x.dtype)

def modulate(h, shift, scale):
    return h * (1.0 + scale) + shift

def swiglu(h, w_gate, w_up, w_down):
    return (jax.nn.silu(h @ w_gate) * (h @ w_up)) @ w_down

def half_ffn(h, shift, scale, gate, g_norm, w_gate, w_up, w_down):
    n = modulate(rmsnorm(h, g_norm), shift, scale)
    return h + 0.5 * gate * swiglu(n, w_gate, w_up, w_down)

def axial_rope(n_tok, d_rot):
    half = d_rot // 2
    freqs = ROPE_THETA ** (-jnp.arange(0, half, 2, dtype=jnp.float32) / half)
    t = jnp.arange(n_tok)
    row = (t // GRID_W).astype(jnp.float32)[:, None] * freqs
    col = (t % GRID_W).astype(jnp.float32)[:, None] * freqs
    ang = jnp.concatenate([row, row, col, col], axis=-1)
    return jnp.cos(ang), jnp.sin(ang)

def apply_rope(x, cos, sin):
    xr = x.reshape(x.shape[:-1] + (2, 2, -1))
    rot = jnp.concatenate([-xr[..., 1:, :], xr[..., :1, :]], axis=-2).reshape(x.shape)
    return x * cos.astype(x.dtype) + rot * sin.astype(x.dtype)

def project_heads(n, w_in, q_norm, k_norm, mq_norm, mkv_norm, w_uq, w_ukv, rope):
    bn, t_len, _ = n.shape
    a_q, a_k, a_v, b_q, b_k, b_v, c_q, c_kv, c_kr, gates = jnp.split(n @ w_in, IN_SPLITS, axis=-1)

    def heads(t, h):
        return t.reshape(bn, t_len, h, -1).transpose(0, 2, 1, 3)

    attn_a = (heads(a_q, NA_HEADS), heads(a_k, NA_HEADS), heads(a_v, NA_HEADS))
    b_q = rmsnorm(heads(b_q, GQA_HEADS), q_norm)
    b_k = rmsnorm(heads(b_k, GQA_KV_HEADS), k_norm)
    q_lat = heads(rmsnorm(c_q, mq_norm) @ w_uq, MLA_HEADS)
    kv_lat = heads(rmsnorm(c_kv, mkv_norm) @ w_ukv, MLA_HEADS)
    q_nope, q_rope = q_lat[..., :MLA_NOPE], q_lat[..., MLA_NOPE:]
    k_nope, m_v = kv_lat[..., :MLA_NOPE], kv_lat[..., MLA_NOPE:]
    k_rope = c_kr[:, None]
    if rope is not None:
        cos_b, sin_b, cos_m, sin_m = rope
        b_q = apply_rope(b_q, cos_b, sin_b)
        b_k = apply_rope(b_k, cos_b, sin_b)
        q_rope = apply_rope(q_rope, cos_m, sin_m)
        k_rope = apply_rope(k_rope, cos_m, sin_m)
    m_q = jnp.concatenate([q_nope, q_rope], axis=-1)
    m_k = jnp.concatenate([k_nope, jnp.broadcast_to(k_rope, k_nope.shape[:-1] + (MLA_ROPE,))], axis=-1)
    return attn_a, (b_q, b_k, heads(b_v, GQA_KV_HEADS)), (m_q, m_k, m_v), gates

def block_attention(q, k, v, scale):
    bn, hq, t_len, dk = q.shape
    hkv = k.shape[1]
    grp = hq // hkv
    nblk = t_len // Q_BLOCK
    qb = q.reshape(bn, hkv, grp, nblk, Q_BLOCK, dk).transpose(3, 0, 1, 2, 4, 5)

    def one_block(qi):
        s = jnp.einsum('bhgqd,bhkd->bhgqk', qi, k).astype(jnp.float32) * scale
        p = jax.nn.softmax(s, axis=-1).astype(v.dtype)
        return jnp.einsum('bhgqk,bhkd->bhgqd', p, v)

    o = lax.map(one_block, qb)
    return o.transpose(1, 2, 3, 0, 4, 5).reshape(bn, hq, t_len, v.shape[-1])

def neighbourhood_attention(q, k, v, k_ctx, v_ctx, rel_bias):
    bn, h, s_len, d = q.shape
    rows = s_len // GRID_W
    wr = min(NA_ROWS, rows)
    scale = d ** -0.5

    def grid(t):
        return t.reshape(bn, h, rows, GRID_W, d)

    kg, vg = grid(k), grid(v)
    q_rows = jnp.moveaxis(grid(q), 2, 0)
    cols = jnp.arange(GRID_W)
    c0 = jnp.clip(cols - NA_COLS // 2, 0, GRID_W - NA_COLS)
    col_in = (cols[None, :] >= c0[:, None]) & (cols[None, :] < c0[:, None] + NA_COLS)
    col_idx = jnp.clip(cols[None, :] - cols[:, None] + NA_COLS - 1, 0, 2 * NA_COLS - 2)
    mask = jnp.broadcast_to(col_in[:, None, :], (GRID_W, wr, GRID_W)).reshape(GRID_W, wr * GRID_W)
    n_loc = wr * GRID_W

    def row_block(args):
        qr, r = args
        r0 = jnp.clip(r - wr // 2, 0, rows - wr)
        kr = lax.dynamic_slice_in_dim(kg, r0, wr, axis=2).reshape(bn, h, n_loc, d)
        vr = lax.dynamic_slice_in_dim(vg, r0, wr, axis=2).reshape(bn, h, n_loc, d)
        dr_idx = r0 + jnp.arange(wr) - r + (NA_ROWS - 1)
        bias = rel_bias[:, dr_idx[None, :, None], col_idx[:, None, :]].reshape(h, GRID_W, n_loc)
        s_loc = jnp.einsum('bhqd,bhkd->bhqk', qr, kr).astype(jnp.float32) * scale + bias.astype(jnp.float32)
        s_loc = jnp.where(mask, s_loc, NEG_BIG)
        s_ctx = jnp.einsum('bhqd,bhkd->bhqk', qr, k_ctx).astype(jnp.float32) * scale
        p = jax.nn.softmax(jnp.concatenate([s_loc, s_ctx], axis=-1), axis=-1).astype(v.dtype)
        return (jnp.einsum('bhqk,bhkd->bhqd', p[..., :n_loc], vr)
                + jnp.einsum('bhqk,bhkd->bhqd', p[..., n_loc:], v_ctx))

    o = lax.map(row_block, (q_rows, jnp.arange(rows)))
    return jnp.moveaxis(o, 0, 2).reshape(bn, h, s_len, d)

def merge_branches(o_a, o_b, o_m, gate_logits, w_a, w_b, w_m, w_o):
    def flat(o):
        return o.transpose(0, 2, 1, 3).reshape(o.shape[0], o.shape[2], -1)

    g_a, g_b, g_m = jnp.split(jax.nn.sigmoid(gate_logits), N_BRANCH, axis=-1)
    y = g_a * (flat(o_a) @ w_a) + g_b * (flat(o_b) @ w_b) + g_m * (flat(o_m) @ w_m)
    return y @ w_o

def setup_inputs(seed: int = 0) -> dict:
    key = jax.random.key(seed)
    ks = iter(jax.random.split(key, 32))
    d = D_MODEL

    def nrm(shape, s):
        return jax.random.normal(next(ks), shape, jnp.float32) * s

    def lin(shape):
        return nrm(shape, shape[-2] ** -0.5)

    def gain(shape):
        return 1.0 + nrm(shape, 0.1)

    return {
        "x": nrm((BATCH, SEQ, d), 1.0),
        "c": nrm((BATCH, d), 1.0),
        "ctx": nrm((BATCH, CTX_LEN, d), 1.0),
        "c_ctx": nrm((d,), 1.0),
        "w_ada": nrm((DEPTH, d, N_MOD * d), 0.5 * d ** -0.5),
        "b_ada": nrm((DEPTH, N_MOD * d), 0.02),
        "ffn1_norm": gain((DEPTH, d)),
        "ffn1_w_gate": lin((DEPTH, d, D_FF)),
        "ffn1_w_up": lin((DEPTH, d, D_FF)),
        "ffn1_w_down": lin((DEPTH, D_FF, d)),
        "mix_norm": gain((DEPTH, d)),
        "w_in": lin((DEPTH, d, IN_WIDTH)),
        "na_rel_bias": nrm((DEPTH, NA_HEADS, 2 * NA_ROWS - 1, 2 * NA_COLS - 1), 0.2),
        "gqa_q_norm": gain((DEPTH, HEAD_DIM)),
        "gqa_k_norm": gain((DEPTH, HEAD_DIM)),
        "mla_q_norm": gain((DEPTH, MLA_Q_RANK)),
        "mla_kv_norm": gain((DEPTH, MLA_KV_RANK)),
        "mla_w_uq": lin((DEPTH, MLA_Q_RANK, MLA_HEADS * (MLA_NOPE + MLA_ROPE))),
        "mla_w_ukv": lin((DEPTH, MLA_KV_RANK, MLA_HEADS * (MLA_NOPE + MLA_V))),
        "w_branch_a": lin((DEPTH, NA_WIDTH, d)),
        "w_branch_b": lin((DEPTH, GQA_Q_WIDTH, d)),
        "w_branch_c": lin((DEPTH, MLA_OUT_WIDTH, d)),
        "w_out": lin((DEPTH, d, d)),
        "ffn2_norm": gain((DEPTH, d)),
        "ffn2_w_gate": lin((DEPTH, d, D_FF)),
        "ffn2_w_up": lin((DEPTH, d, D_FF)),
        "ffn2_w_down": lin((DEPTH, D_FF, d)),
        "final_norm": gain((d,)),
    }

def reference(x, c, ctx, c_ctx, w_ada, b_ada, ffn1_norm, ffn1_w_gate, ffn1_w_up, ffn1_w_down,
              mix_norm, w_in, na_rel_bias, gqa_q_norm, gqa_k_norm, mla_q_norm, mla_kv_norm,
              mla_w_uq, mla_w_ukv, w_branch_a, w_branch_b, w_branch_c, w_out,
              ffn2_norm, ffn2_w_gate, ffn2_w_up, ffn2_w_down, final_norm):
    n_tok = x.shape[1]
    cos_b, sin_b = axial_rope(n_tok, HEAD_DIM)
    cos_m, sin_m = axial_rope(n_tok, MLA_ROPE)
    rope = (cos_b, sin_b, cos_m, sin_m)
    na_scale = HEAD_DIM ** -0.5
    gqa_scale = HEAD_DIM ** -0.5
    mla_scale = (MLA_NOPE + MLA_ROPE) ** -0.5

    for i in range(DEPTH):
        mod_x = [m[:, None, :] for m in jnp.split(jax.nn.silu(c) @ w_ada[i] + b_ada[i], N_MOD, axis=-1)]
        mod_c = jnp.split(jax.nn.silu(c_ctx) @ w_ada[i] + b_ada[i], N_MOD, axis=-1)
        ffn1 = (ffn1_norm[i], ffn1_w_gate[i], ffn1_w_up[i], ffn1_w_down[i])
        ffn2 = (ffn2_norm[i], ffn2_w_gate[i], ffn2_w_up[i], ffn2_w_down[i])
        proj = (w_in[i], gqa_q_norm[i], gqa_k_norm[i], mla_q_norm[i], mla_kv_norm[i], mla_w_uq[i], mla_w_ukv[i])
        merge = (w_branch_a[i], w_branch_b[i], w_branch_c[i], w_out[i])

        x = half_ffn(x, mod_x[0], mod_x[1], mod_x[2], *ffn1)
        ctx = half_ffn(ctx, mod_c[0], mod_c[1], mod_c[2], *ffn1)

        nx = modulate(rmsnorm(x, mix_norm[i]), mod_x[3], mod_x[4])
        nc = modulate(rmsnorm(ctx, mix_norm[i]), mod_c[3], mod_c[4])
        (aq, ak, av), (bq, bk, bv), (mq, mk, mv), gates = project_heads(nx, *proj, rope)
        (caq, cak, cav), (cbq, cbk, cbv), (cmq, cmk, cmv), cgates = project_heads(nc, *proj, None)

        o_a = neighbourhood_attention(aq, ak, av, cak, cav, na_rel_bias[i])
        o_b = block_attention(bq, jnp.concatenate([bk, cbk], axis=2), jnp.concatenate([bv, cbv], axis=2), gqa_scale)
        o_m = block_attention(mq, jnp.concatenate([mk, cmk], axis=2), jnp.concatenate([mv, cmv], axis=2), mla_scale)
        x = x + mod_x[5] * merge_branches(o_a, o_b, o_m, gates, *merge)
        x = half_ffn(x, mod_x[6], mod_x[7], mod_x[8], *ffn2)

        if i < DEPTH - 1:
            oc_a = block_attention(caq, cak, cav, na_scale)
            oc_b = block_attention(cbq, cbk, cbv, gqa_scale)
            oc_m = block_attention(cmq, cmk, cmv, mla_scale)
            ctx = ctx + mod_c[5] * merge_branches(oc_a, oc_b, oc_m, cgates, *merge)
            ctx = half_ffn(ctx, mod_c[6], mod_c[7], mod_c[8], *ffn2)

    return rmsnorm(x, final_norm)


_drawn_inputs = setup_inputs


def setup_inputs(seed=0):
    import zlib

    import numpy as np

    out = dict(_drawn_inputs(seed))
    spreads = {}
    factors = {'b_ada': 2.879,
     'mix_norm': 6.501,
     'na_rel_bias': 8.0,
     'gqa_q_norm': 8.0,
     'gqa_k_norm': 8.0,
     'mla_q_norm': 8.0,
     'mla_kv_norm': 8.0,
     'ffn2_norm': 2.795}
    for name, (base, spread) in spreads.items():
        noise = np.random.default_rng([zlib.crc32(name.encode()), seed]).standard_normal(out[name].shape)
        drawn = base * np.exp(spread * noise) if base else spread * noise
        out[name] = jnp.asarray(drawn.astype(out[name].dtype))
    for name, factor in factors.items():
        out[name] = (out[name] * factor).astype(out[name].dtype)
    return out
```

```python
from contextlib import ExitStack

import concourse.bass as bass
from concourse import mybir

F32 = mybir.dt.float32
F32R = mybir.dt.float32r
I32 = mybir.dt.int32
ACT = mybir.ActivationFunctionType
ALU = mybir.AluOpType
AX = mybir.AxisListType

P = 128
D_MODEL = 1024
DEPTH = 2
TX = 256
T = 512
KT = D_MODEL // P
D_FF = ((8 * D_MODEL // 3 + 127) // 128) * 128
FT = D_FF // P
GROUPS = (8, 8, 6)
GRID_W = 64
N_MOD = 9
EPS = 1e-6
HD = 64
ROPE_M = 32
MW = HD + ROPE_M
NA_SCALE = HD ** -0.5
MLA_SCALE = MW ** -0.5
RSQRT_MAGIC = 1597463007.0
NA_DR, NA_DC = 15, 31
UNIT = 16 * P

UP_OFF = (0, 12, 24)
DOWN_OFF = (8, 20, 30)
FFN_UNITS = 34
MIX_SIZES = (2048, 2048, 2048, 2048, 8 * P + 8 * MW, 2 * 4 * MW, 512, 2048, 2048, 2048)
MIX_UNITS = len(MIX_SIZES)
MERGE_UNITS = 2 * KT
OUT_UNITS = KT // 2
MIX0 = FFN_UNITS
MERGE0 = MIX0 + MIX_UNITS
OUT0 = MERGE0 + MERGE_UNITS
FFN2_0 = OUT0 + OUT_UNITS
LAYER_UNITS = FFN2_0 + FFN_UNITS
TOTAL_UNITS = DEPTH * LAYER_UNITS
VISITS = (3 * KT, KT, 3 * KT)
LAYER_VISITS = sum(VISITS)

PIECES = DEPTH * N_MOD * D_MODEL // 512
LP = PIECES // DEPTH
EARLY_PIECES = 4
ADA_UP = {(0, 0): 4, (0, 1): 10, (0, 2): 14, (1, 0): 17, (1, 1): 21, (1, 2): 25, (2, 0): 28, (2, 1): 32}
ADA_DOWN = {(0, 0): 8}


def _pieces_before(f):
    return (EARLY_PIECES + sum(GROUPS[g] // 2 for (h, g) in ADA_UP if h < f) + sum(2 for (h, g) in ADA_DOWN if h < f))


PIECES_BY_NORM = [_pieces_before(2 * (r // 3) + (r % 3 > 0)) for r in range(3 * DEPTH)] + [PIECES]

G_FFN1, G_MIX, G_FFN2, G_CQ, G_CKV, G_Q, G_K = 0, 8, 16, 24, 26, 27, 28
G_LAYER = 29
G_FINAL = DEPTH * G_LAYER
G_C = G_FINAL + KT
G_BADA = G_C + 2 * KT
G_WIDTH = G_BADA + DEPTH * N_MOD * KT
C_ID, C_ONES, C_SEL0, C_SEL1, C_ROTB, C_ROTM, C_MASK, C_COSB, C_SINB, C_COSM, C_SINM, C_COL = (
    0, 128, 256, 384, 512, 640, 768, 1024, 1280, 1536, 1792, 2048)
C_WIDTH = C_COL + 6
COL_MODEL, COL_HEAD, COL_CQ, COL_CKV, COL_ONE = 0, 1, 3, 4, 5

ST_K, ST_CKV, ST_CQ, ST_Q = 0, 2, 3, 4


def build(nc, dram, out):
    ctx = ExitStack()
    with ctx:
        def sb(name, shape, dt=F32, scope=ctx):
            return scope.enter_context(nc.sbuf_tensor(name, shape, dt))

        def sem(name):
            return ctx.enter_context(nc.semaphore(name))

        x = sb("x", [P, KT, T])
        n_hi = sb("n_hi", [P, KT, T], F32R)
        n_lo = sb("n_lo", [P, KT, T], F32R)
        h_hi = sb("h_hi", [P, 8, T], F32R)
        h_lo = sb("h_lo", [P, 8, T], F32R)
        w_raw = [sb(f"w_raw{s}", [P, UNIT]) for s in range(2)]
        w_hi = [sb(f"w_hi{s}", [P, UNIT], F32R) for s in range(2)]
        w_lo = [sb(f"w_lo{s}", [P, UNIT], F32R) for s in range(2)]
        tmp = sb("tmp", [P, 6, T])
        probs = sb("probs", [P, 2, 2, T])
        const = sb("const_sb", [P, C_WIDTH])
        gains = sb("gains_sb", [P, G_WIDTH])
        silu_c = sb("silu_c", [P, 2 * KT])
        mods = sb("mods", [P, 2, DEPTH * N_MOD * KT])
        coef_a = sb("coef_a", [P, 2, KT])
        coef_g = sb("coef_g", [P, 2, KT])
        rstd = sb("rstd", [P, 48])
        rs_v = sb("rs_v", [P, 48])
        rs_a = sb("rs_a", [P, 48])
        rs_b = sb("rs_b", [P, 48])
        qscale = sb("qscale", [P, 36])
        mx = sb("mx", [P, 2, 2])
        nbias = sb("nbias", [P, 2, 2])
        rsum = sb("rsum", [P, 2, 2])
        rinv = sb("rinv", [P, 2, 2])
        with ExitStack() as s:
            bq = sb("bq", [P, 4, T], F32, s)
            bk = sb("bk", [P, T], F32, s)
            aq = sb("aq", [P, 2, T], F32, s)
            ak = sb("ak", [P, 2, T], F32, s)
            mq = sb("mq", [P, 4, T], F32, s)
            mk = sb("mk", [P, 4, T], F32, s)
            val = sb("val", [P, 4, 640], F32, s)
        with ExitStack() as s:
            sq_sum = sb("sq_sum", [P, T], F32, s)
            y_hi = sb("y_hi", [P, KT, T], F32R, s)
            y_lo = sb("y_lo", [P, KT, T], F32R, s)
        with ExitStack() as s:
            sb("below_ada", [P, T], F32, s)
            ada_raw = [sb(f"ada_raw{i}", [P, 4, 512], F32, s) for i in range(2)]
            ada_acc = sb("ada_acc", [P, 2, 512], F32, s)
            staged = sb("staged", [P, KT, TX], F32, s)

        bank = ctx.enter_context(nc.psum_tensor("bank", [P, 8, 512], F32))
        STAT, BCAST = 6, 7

        squares = [probs[:, 1, i, :] for i in range(2)]
        diag = [probs[:, 0, i, :] for i in range(2)]
        ident = const[:, C_ID:C_ID + P]
        ones = const[:, C_ONES:C_ONES + P]

        def col(i, n=1):
            return const[:, C_COL + i:C_COL + i + n]

        s_const = sem("s_const")
        s_x = sem("s_x")
        raw_in = [sem(f"raw_in{i}") for i in range(2)]
        hi_done = sem("hi_done")
        lo_done = sem("lo_done")
        units_done = sem("units_done")
        ada_in = [sem(f"ada_in{i}") for i in range(2)]
        ada_used = sem("ada_used")
        ada_step = sem("ada_step")
        ada_cols = sem("ada_cols")
        ada_done = sem("ada_done")
        sq_done = sem("sq_done")
        sq_added = sem("sq_added")
        stat_ready = sem("stat_ready")
        diag_ready = sem("diag_ready")
        bcast_ready = sem("bcast_ready")
        scaled = sem("scaled")
        modulated = sem("modulated")
        n_hi_done = sem("n_hi_done")
        n_ready = sem("n_ready")
        tanh_done = sem("tanh_done")
        silu_done = sem("silu_done")
        gu_used = sem("gu_used")
        h_hi_done = sem("h_hi_done")
        h_lo_done = sem("h_lo_done")
        y_even = sem("y_even")
        x_done = sem("x_done")
        proj_mid = sem("proj_mid")
        proj_used = sem("proj_used")
        msq_ready = sem("msq_ready")
        msq_used = sem("msq_used")
        rot_ready = sem("rot_ready")
        rot_used = sem("rot_used")
        mstat_used = sem("mstat_used")
        mdiag_ready = sem("mdiag_ready")
        mbc_ready = sem("mbc_ready")
        lat_f32 = sem("lat_f32")
        lat_hi = sem("lat_hi")
        lat_lo = sem("lat_lo")
        kv_ready = sem("kv_ready")
        bias_in = [sem(f"bias_in{i}") for i in range(2)]
        bias_used = sem("bias_used")
        s_ready = sem("s_ready")
        nb_ready = sem("nb_ready")
        exp_done = sem("exp_done")
        p_ready = sem("p_ready")
        pt_ready = sem("pt_ready")
        pt_a = sem("pt_a")
        pt_b = sem("pt_b")
        o_ready = sem("o_ready")
        o_hi = sem("o_hi")
        o_lo = sem("o_lo")
        mg_ready = sem("mg_ready")
        mg_tanh = sem("mg_tanh")
        mg_used = sem("mg_used")
        mg_add = sem("mg_add")
        mg_y = sem("mg_y")
        yh_done = sem("yh_done")
        yl_done = sem("yl_done")
        a_step = sem("a_step")
        v_step = sem("v_step")
        fin_t = sem("fin_t")
        fin_o = sem("fin_o")
        s_out = sem("s_out")

        def ffn_base(f):
            return (f // 2) * LAYER_UNITS + (f % 2) * FFN2_0

        def visit_base(layer, phase):
            return layer * LAYER_VISITS + sum(VISITS[:phase])

        def width(f):
            return TX if f == 2 * DEPTH - 1 else T

        def tile_of(t, i, w=T, at=0):
            return t[:, bass.ds(i, 1), at:at + w].rearrange("p a b -> p (a b)")

        def blocks(layer):
            parts = (0, 1) if layer < DEPTH - 1 else (0,)
            found = []
            for tile in range(8):
                for half in range(2):
                    for part in parts:
                        kind, t = ("a", tile) if tile < 2 else ("b", tile - 2) if tile < 6 else ("m", tile - 6)
                        found.append((kind, t, half, part, tile, half == 1 and part == parts[-1]))
            return found

        N_BLOCKS = [len(blocks(i)) for i in range(DEPTH)]
        A_BLOCKS = [sum(b[0] == "a" for b in blocks(i)) for i in range(DEPTH)]

        def block_base(layer):
            return sum(N_BLOCKS[:layer])

        def x_blocks(layer, n):
            return sum(b[3] == 0 for b in blocks(layer)[:n])

        PROJ = [("bq", 0), ("bq", 1), ("bq", 2), ("bq", 3), ("bk", 0), ("ckv", 0), ("cq", 0), ("cq", 1),
                ("vb", 0), ("kr", 0), ("mq", 0), ("mq", 1), ("mq", 2), ("mq", 3),
                ("mk", 0), ("mk", 1), ("mk", 2), ("mk", 3), ("vm", 0), ("vm", 1),
                ("ak", 0), ("ak", 1), ("aq", 0), ("aq", 1), ("va", 0), ("va", 1)]
        PROJ_UNIT = [0, 0, 1, 1, 2, 2, 3, 3, 4, 4, 5, 5, 5, 5, 6, 6, 6, 6, 6, 6, 7, 7, 8, 8, 9, 9]
        N_PROJ = len(PROJ)

        def proj_last(j):
            return j + 1 == N_PROJ or PROJ_UNIT[j + 1] != PROJ_UNIT[j]

        def wait_proj(e, layer, j):
            if proj_last(j):
                e.wait_ge(units_done, layer * LAYER_UNITS + MIX0 + PROJ_UNIT[j] + 3)
            else:
                mids = sum(not proj_last(i) for i in range(N_PROJ))
                e.wait_ge(proj_mid, layer * mids + sum(not proj_last(i) for i in range(j + 1)))

        ROT = [("bq", 0), ("bq", 1), ("bq", 2), ("bq", 3), ("bk", 0), ("kr", 0),
               ("mq", 0), ("mq", 1), ("mq", 2), ("mq", 3)]
        N_ROT = len(ROT)

        block = ctx.enter_context(nc.Block())

        @block.sync
        def _(sp):
            def load(unit, slot, src, size=UNIT):
                sp.wait_ge(lo_done, unit + 1)
                sp.dma_start(w_raw[slot][:, 0:size], src).then_inc(raw_in[slot], 16)

            def load_ada(piece):
                for half in range(2):
                    sp.wait_ge(ada_used, 2 * piece + half + 1)
                    sp.dma_start(ada_raw[half][:, :, :], dram["w_ada"][piece, half]).then_inc(ada_in[half], 16)

            def load_ffn(f):
                base = ffn_base(f)
                start = 0
                for g, n in enumerate(GROUPS):
                    with sp.Fori(0, n // 2) as i:
                        for s in range(2):
                            load(base + UP_OFF[g] + 2 * i + s, s, dram["w_up"][f, start + 2 * i + s])
                        if (f, g) in ADA_UP:
                            if f % 2 and g == 0:
                                sp.wait_ge(units_done, base + 2)
                            load_ada(ADA_UP[f, g] + i)
                    src = dram["w_down"] if n == 8 else dram["w_down_last"]
                    with sp.Fori(0, 2) as i:
                        for s in range(2):
                            at = src[f, g, 2 * i + s] if n == 8 else src[f, 2 * i + s]
                            load(base + DOWN_OFF[g] + 2 * i + s, s, at, 2 * n * P)
                        if (f, g) in ADA_DOWN:
                            load_ada(ADA_DOWN[f, g] + i)
                    start += n

            sp.dma_start(gains[:, :], dram["gains"]).then_inc(s_const, 16)
            sp.dma_start(const[:, :], dram["const"]).then_inc(s_const, 16)
            load_ada(0)
            sp.dma_start(x[:, :, :], dram["x_t"]).then_inc(s_x, 16)
            for piece in range(1, EARLY_PIECES):
                load_ada(piece)
            for layer in range(DEPTH):
                load_ffn(2 * layer)
                base = layer * LAYER_UNITS
                at = 0
                for u, size in enumerate(MIX_SIZES):
                    load(base + MIX0 + u, u % 2, dram["w_mix"][layer, :, at:at + size], size)
                    at += size
                with sp.Fori(0, KT) as i:
                    for s in range(2):
                        load(base + MERGE0 + 2 * i + s, s, dram["w_merge"][layer, 2 * i + s])
                with sp.Fori(0, OUT_UNITS // 2) as i:
                    for s in range(2):
                        load(base + OUT0 + 2 * i + s, s, dram["w_out"][layer, 2 * i + s])
                load_ffn(2 * layer + 1)
            for part in range(2):
                sp.wait_ge(fin_o, 4 * (part + 1))
                sp.dma_start(out[:, 4 * part:4 * part + 4, :], staged[:, 4 * part:4 * part + 4, :]).then_inc(s_out, 16)
            sp.wait_ge(s_out, 32)

        @block.gpsimd
        def _(pool):
            pool.sem_inc(lo_done, 2)
            with pool.Fori(0, TOTAL_UNITS // 2) as i:
                for s in range(2):
                    pool.wait_ge(hi_done, 2 * i + s + 1)
                    pool.tensor_tensor(w_lo[s][:, :], w_raw[s][:, :], w_hi[s][:, :].bitcast(F32),
                                       ALU.subtract).then_inc(lo_done, 1)

        @block.scalar
        def _(act):
            steps = [0]

            def then(ins):
                steps[0] += 1
                ins.then_inc(a_step, 1)
                act.wait_ge(a_step, steps[0])

            def split_hi(unit, slot, turn):
                act.wait_ge(units_done, unit + 1)
                act.wait_ge(raw_in[slot], 16 * (turn + 1))
                act.activation(w_hi[slot][:, :], w_raw[slot][:, :], ACT.Copy).then_inc(hi_done, 1)

            def next_hi(base, i, s):
                split_hi(base + 2 * i + s + 2, s, base // 2 + i + 1)

            def square(visit, q, dt, w, parity):
                act.wait_ge(x_done, visit + 3)
                act.wait_ge(sq_added, q + 1)
                act.activation(squares[parity][:, 0:w], tile_of(x, dt, w), ACT.Square).then_inc(sq_done, 1)

            def norm(r, layer, m, w):
                for dt in range(KT):
                    at = layer * N_MOD * KT + m * KT + dt
                    act.wait_ge(scaled, 8 * r + dt + 1)
                    if 8 * r + dt >= 2:
                        act.wait_ge(n_ready, 8 * r + dt - 1)
                    for v in range(w // TX):
                        ins = act.activation(tmp[:, 2 + dt % 2, v * TX:(v + 1) * TX], tmp[:, dt % 2, v * TX:(v + 1) * TX],
                                             ACT.Identity, scale=coef_a[:, v, dt:dt + 1], bias=mods[:, v, at:at + 1])
                    ins.then_inc(modulated, 1)
                    act.wait_ge(modulated, 8 * r + dt + 1)
                    act.activation(n_hi[:, dt, 0:w], tmp[:, 2 + dt % 2, 0:w], ACT.Copy).then_inc(n_hi_done, 1)

            def ffn(f, q0):
                w, base, layer = width(f), ffn_base(f), f // 2
                start = 0
                for g, n in enumerate(GROUPS):
                    ub, db = base + UP_OFF[g], base + DOWN_OFF[g]
                    vb = visit_base(layer, 2 * (f % 2)) + g * KT
                    last = f == 2 * DEPTH - 1 and g == 2
                    with act.Fori(0, n // 2) as i:
                        for s in range(2):
                            tile = FT * f + start + 2 * i + s
                            next_hi(ub, i, s)
                            act.wait_ge(units_done, ub + 2 * i + s + 3)
                            act.activation(tmp[:, s, 0:w], bank[:, 2 * s, 0:w], ACT.Tanh, scale=0.5).then_inc(tanh_done, 1)
                            act.wait_ge(gu_used, tile + 3)
                            act.activation(tile_of(h_hi, 2 * i + s, w), tmp[:, 4 + s, 0:w], ACT.Copy).then_inc(h_hi_done, 1)
                    if g < 2:
                        with act.Fori(0, 2) as i:
                            for s in range(2):
                                next_hi(db, i, s)
                    elif not last:
                        with act.Fori(0, 2) as i:
                            for s in range(2):
                                next_hi(db, i, s)
                                for d in range(2):
                                    square(vb + 4 * i + 2 * s + d, q0 + 4 * i + 2 * s + d, 4 * i + 2 * s + d, w, d)
                    else:
                        for i in range(2):
                            for s in range(2):
                                if i == 0:
                                    next_hi(db, i, s)
                                for d in range(2):
                                    square(vb + 4 * i + 2 * s + d, q0 + 4 * i + 2 * s + d, 4 * i + 2 * s + d, w, d)
                    start += n

            def project(layer):
                wq = T if layer < DEPTH - 1 else TX
                base = layer * LAYER_UNITS + MIX0
                g0 = layer * G_LAYER
                for h in range(2):
                    load_bias(layer, h)
                n_sq = n_lat = 0
                for j, (kind, t) in enumerate(PROJ):
                    src = bank[:, j % 4, :]
                    wait_proj(act, layer, j)
                    if proj_last(j):
                        u = PROJ_UNIT[j]
                        next_hi(base + u - u % 2, 0, u % 2)
                    w = wq if kind in ("bq", "cq", "mq", "aq") else T
                    if kind in ("bq", "bk", "ckv", "cq"):
                        k = 8 * layer + n_sq
                        if k >= 2:
                            act.wait_ge(msq_used, k - 1)
                        act.activation(squares[n_sq % 2][:, 0:w], src[:, 0:w], ACT.Square).then_inc(msq_ready, 1)
                        n_sq += 1
                    if kind == "bq":
                        act.activation(bq[:, t, 0:w], src[:, 0:w], ACT.Copy,
                                       scale=gains[:, g0 + G_Q:g0 + G_Q + 1]).then_inc(proj_used, 1)
                    elif kind == "bk":
                        act.activation(bk[:, :], src, ACT.Copy, scale=gains[:, g0 + G_K:g0 + G_K + 1]).then_inc(proj_used, 1)
                    elif kind == "ckv":
                        act.activation(tmp[:, 0, :], src, ACT.Copy, scale=gains[:, g0 + G_CKV:g0 + G_CKV + 1]).then_inc(proj_used, 1)
                    elif kind == "cq":
                        g = g0 + G_CQ + t
                        act.activation(tmp[:, 1 + t, 0:w], src[:, 0:w], ACT.Copy, scale=gains[:, g:g + 1]).then_inc(proj_used, 1)
                        act.wait_ge(proj_used, N_PROJ * layer + j + 1)
                        act.activation(h_hi[:, t, 0:w], tmp[:, 1 + t, 0:w], ACT.Copy).then_inc(lat_hi, 1)
                    elif kind == "vb":
                        act.activation(val[:, :, 256:384], src.rearrange("p (j c) -> p j c", j=4), ACT.Copy).then_inc(proj_used, 1)
                    elif kind == "vm":
                        act.activation(val[:, 2 * t:2 * t + 2, 384:640], src.rearrange("p (j c) -> p j c", j=2),
                                       ACT.Copy).then_inc(proj_used, 1)
                    elif kind == "va":
                        act.activation(val[:, 2 * t:2 * t + 2, 0:256], src.rearrange("p (j c) -> p j c", j=2),
                                       ACT.Copy).then_inc(proj_used, 1)
                    elif kind == "kr":
                        act.activation(mk[64:96, 0, :], src[64:96, :], ACT.Copy).then_inc(proj_used, 1)
                        act.wait_ge(lat_f32, layer + 1)
                        act.activation(h_hi[:, 2, :], tmp[:, 0, :], ACT.Copy).then_inc(lat_hi, 1)
                    elif kind == "mk":
                        act.activation(mk[0:64, t, :], src[0:64, :], ACT.Copy).then_inc(proj_used, 1)
                    else:
                        rows = 96 if kind == "mq" else 128
                        dst = {"mq": mq, "ak": ak, "aq": aq}[kind]
                        act.activation(dst[0:rows, t, 0:w], src[0:rows, 0:w], ACT.Copy).then_inc(proj_used, 1)
                act.wait_ge(rot_used, N_ROT * layer + 6)
                for t in range(1, 4):
                    act.activation(mk[64:96, t, :], mk[64:96, 0, :], ACT.Copy).then_inc(kv_ready, 1)

            def load_bias(layer, h):
                for qr in range(4):
                    src = bass.AP(dram["rel_bias"].tensor, ((layer * 4 + h) * NA_DR + 7 - qr) * GRID_W * NA_DC + 15,
                                  [[NA_DC - 1, GRID_W], [GRID_W * NA_DC, 4], [1, GRID_W]])
                    dst = tmp[64 * (qr % 2):64 * (qr % 2) + 64, 4 + h % 2, (qr // 2) * 256:(qr // 2) * 256 + 256]
                    act.dma_start(dst.rearrange("p (a b) -> p a b", a=4), src).then_inc(bias_in[h % 2], 16)

            def attention(layer):
                todo = blocks(layer)
                b0 = block_base(layer)
                na_seen = 0

                def exps(n):
                    kind, t, half, part, tile, _ = todo[n]
                    keys = T if part == 0 else TX
                    act.wait_ge(nb_ready, b0 + n + 1)
                    for q in range(2):
                        j = 2 * part + q
                        c = {"b": 4 * (1 + 2 * t + half), "m": 0, "a": 0}[kind] + j
                        scale = NA_SCALE if kind == "a" else qscale[:, c:c + 1]
                        ins = act.activation(probs[:, n % 2, q, 0:keys], bank[:, 2 * (n % 2) + q, 0:keys], ACT.Exp,
                                             bias=nbias[:, n % 2, q:q + 1], scale=scale,
                                             accum_out=rsum[:, n % 2, q:q + 1])
                    ins.then_inc(exp_done, 1)
                    if kind == "a" and part == 0 and tile == 0:
                        h = half + 2
                        act.wait_ge(bias_used, 4 * layer + half + 1)
                        load_bias(layer, h)

                def out_hi(n):
                    tile = todo[n][4]
                    w = T if layer < DEPTH - 1 else TX
                    act.wait_ge(o_ready, 8 * layer + tile + 1)
                    act.activation(h_hi[:, tile, 0:w], bank[:, 6 + tile % 2, 0:w], ACT.Copy).then_inc(o_hi, 1)

                exps(0)
                exps(1)
                for n in range(len(todo)):
                    part = todo[n][3]
                    act.wait_ge(pt_ready, b0 + n + 1)
                    act.activation(tmp[:, 2 * (n % 2), :], bank[:, 4, :], ACT.Copy).then_inc(pt_a, 1)
                    if n and todo[n - 1][5]:
                        out_hi(n - 1)
                    if n + 2 < len(todo):
                        exps(n + 2)
                out_hi(len(todo) - 1)

            def merge(layer):
                w = T if layer < DEPTH - 1 else TX
                base = layer * LAYER_UNITS + MERGE0
                m0 = layer * KT
                with act.Fori(0, KT) as i:
                    d = m0 + i
                    act.wait_ge(mg_used, 3 * d + 3)
                    act.wait_ge(mg_ready, 4 * d + 1)
                    act.activation(tmp[:, 0, 0:w], bank[:, 0, 0:w], ACT.Tanh, scale=0.5).then_inc(mg_tanh, 1)
                    next_hi(base, i, 0)
                    act.activation(tmp[:, 1, 0:w], bank[:, 1, 0:w], ACT.Tanh, scale=0.5).then_inc(mg_tanh, 1)
                    act.wait_ge(mg_ready, 4 * d + 2)
                    act.activation(tmp[:, 2, 0:w], bank[:, 2, 0:w], ACT.Tanh, scale=0.5).then_inc(mg_tanh, 1)
                    next_hi(base, i, 1)
                    act.wait_ge(mg_y, d + 1)
                    act.activation(tile_of(y_hi, i, w), tmp[:, 4, 0:w], ACT.Copy).then_inc(yh_done, 1)
                base = layer * LAYER_UNITS + OUT0
                vb = visit_base(layer, 1)
                q0 = 8 + 24 * layer + 8
                with act.Fori(0, OUT_UNITS // 2) as i:
                    for s in range(2):
                        next_hi(base, i, s)
                        for d in range(2):
                            square(vb + 4 * i + 2 * s + d, q0 + 4 * i + 2 * s + d, 4 * i + 2 * s + d, w, d)

            act.sem_inc(mg_tanh, 3)
            act.wait_ge(s_const, 32)
            then(act.activation(rs_a[:, 0:2 * KT], gains[:, G_C:G_C + 2 * KT], ACT.Tanh, scale=0.5))
            for dt in range(KT):
                if dt == 0:
                    act.wait_ge(s_x, 16)
                act.wait_ge(sq_added, dt + 1)
                act.activation(squares[dt % 2], x[:, dt, :], ACT.Square).then_inc(sq_done, 1)
            for s in range(2):
                split_hi(s, s, 0)
            for layer in range(DEPTH):
                r = 3 * layer
                w = T if layer < DEPTH - 1 else TX
                norm(r, layer, 0, T)
                ffn(2 * layer, 8 + 24 * layer)
                norm(r + 1, layer, 3, T)
                project(layer)
                attention(layer)
                merge(layer)
                norm(r + 2, layer, 6, w)
                ffn(2 * layer + 1, 8 + 24 * layer + 16)
            for dt in range(KT):
                act.wait_ge(fin_t, dt + 1)
                act.activation(staged[:, dt, :], tmp[:, dt % 2, 0:TX], ACT.Copy,
                               scale=gains[:, G_FINAL + dt:G_FINAL + dt + 1]).then_inc(fin_o, 1)

        @block.tensor
        def _(pe):
            def split_product(dst, wh, wl, ah, al, first, last):
                pe.matmul(dst, wh, ah, start=first, stop=False)
                pe.matmul(dst, wh, al, start=False, stop=False)
                return pe.matmul(dst, wl, ah, start=False, stop=last)

            def wblock(slot, at, m=P):
                return w_hi[slot][:, at:at + m], w_lo[slot][:, at:at + m]

            def reduce_ada(piece):
                pe.wait_ge(ada_step, 16 * (piece + 1))
                for v in range(2):
                    for m in range(4):
                        ins = pe.matmul(bank[:, STAT, 4 * v + m:4 * v + m + 1], ada_acc[:, v, m * P:(m + 1) * P],
                                        col(COL_ONE), start=True, stop=True)
                ins.then_inc(ada_cols, 1)

            def norm(r, w):
                pe.wait_ge(ada_done, PIECES_BY_NORM[r])
                if r % 3 == 2:
                    pe.wait_ge(mstat_used, 2 * (r // 3 + 1))
                pe.wait_ge(sq_added, 8 * (r + 1) + 2)
                for j in range(w // P):
                    ins = pe.matmul(bank[:, STAT, j:j + 1], sq_sum[:, j * P:(j + 1) * P], col(COL_MODEL),
                                    start=True, stop=True)
                ins.then_inc(stat_ready, 1)
                pe.wait_ge(diag_ready, r + 1)
                pe.matmul(bank[:, BCAST, 0:w], ones, diag[0][:, 0:w], start=True, stop=True).then_inc(bcast_ready, 1)

            def down(ub, vb, n, a_hi, a_lo, w, wait, extra=None):
                with pe.Fori(0, 2) as i:
                    for s in range(2):
                        pe.wait_ge(lo_done, ub + 2 * i + s + 3)
                        for d in range(2):
                            pe.wait_ge(x_done, vb + 4 * i + 2 * s + d + 1)
                            for k in range(n):
                                if s == 0 and d == 0:
                                    wait(k)
                                wh, wl = wblock(s, (d * n + k) * P)
                                ins = split_product(bank[:, 4 + d, 0:w], wh, wl, a_hi[:, k, 0:w], a_lo[:, k, 0:w],
                                                    k == 0, k == n - 1)
                            ins.then_inc(units_done if d else y_even, 1)
                    if extra is not None:
                        reduce_ada(extra + i)

            def ffn(f, r):
                w, base, layer = width(f), ffn_base(f), f // 2
                start = 0
                for g, n in enumerate(GROUPS):
                    ub = base + UP_OFF[g]
                    with pe.Fori(0, n // 2) as i:
                        for s in range(2):
                            pe.wait_ge(lo_done, ub + 2 * i + s + 3)
                            pe.wait_ge(gu_used, FT * f + start + 2 * i + s + 1)
                            for m in range(2):
                                for k in range(KT):
                                    if g == 0 and s == 0 and m == 0:
                                        pe.wait_ge(n_ready, 8 * r + k + 1)
                                    wh, wl = wblock(s, (m * KT + k) * P)
                                    ins = split_product(bank[:, 2 * s + m, 0:w], wh, wl, n_hi[:, k, 0:w], n_lo[:, k, 0:w],
                                                        k == 0, k == KT - 1)
                            ins.then_inc(units_done, 1)
                        if (f, g) in ADA_UP:
                            reduce_ada(ADA_UP[f, g] + i)
                    start += n

                    def hidden_ready(k, n=n, start=start):
                        if k == 0:
                            pe.wait_ge(h_lo_done, FT * f + start - 2)
                        elif k >= n - 2:
                            pe.wait_ge(h_lo_done, FT * f + start - (n - 1 - k))

                    down(base + DOWN_OFF[g], visit_base(layer, 2 * (f % 2)) + g * KT, n, h_hi, h_lo, w, hidden_ready,
                         ADA_DOWN.get((f, g)))

            def project(layer, r):
                wq = T if layer < DEPTH - 1 else TX
                base = layer * LAYER_UNITS + MIX0
                rots = [0]
                n_sq = 0

                def rotate(lhs, rhs):
                    m = N_ROT * layer + rots[0]
                    if m >= 2:
                        pe.wait_ge(rot_used, m - 1)
                    pe.matmul(bank[0:lhs.shape[1], 4 + rots[0] % 2, 0:TX], lhs, rhs, start=True, stop=True).then_inc(rot_ready, 1)
                    rots[0] += 1

                def head_stats(k, c, w, sel):
                    pe.wait_ge(msq_ready, 8 * layer + k + 1)
                    for j in range(w // P):
                        dst = bank[:, STAT, 4 * c + j:4 * c + j + 5:4]
                        ins = pe.matmul(dst, squares[k % 2][:, j * P:(j + 1) * P], sel, start=True, stop=True)
                    ins.then_inc(msq_used, 1)

                def after(j):
                    kind, t = PROJ[j]
                    if kind == "bq":
                        head_stats(t, ST_Q + 2 * t, wq, col(COL_HEAD, 2))
                        pe.wait_ge(proj_used, N_PROJ * layer + j + 1)
                        rotate(const[:, C_ROTB:C_ROTB + P], bq[:, t, 0:TX])
                    elif kind == "bk":
                        head_stats(4, ST_K, T, col(COL_HEAD, 2))
                        pe.wait_ge(proj_used, N_PROJ * layer + j + 1)
                        rotate(const[:, C_ROTB:C_ROTB + P], bk[:, 0:TX])
                    elif kind == "ckv":
                        pe.wait_ge(msq_ready, 8 * layer + 6)
                        for i in range(4):
                            ins = pe.matmul(bank[:, STAT, 4 * ST_CKV + i:4 * ST_CKV + i + 1], squares[1][:, i * P:(i + 1) * P],
                                            col(COL_CKV), start=True, stop=True)
                        ins.then_inc(msq_used, 1)
                    elif kind == "cq" and t == 1:
                        pe.wait_ge(msq_ready, 8 * layer + 8)
                        pe.wait_ge(mstat_used, 2 * layer + 1)
                        for i in range(wq // P):
                            for c in range(2):
                                ins = pe.matmul(bank[:, STAT, 4 * ST_CQ + i:4 * ST_CQ + i + 1],
                                                squares[c][:, i * P:(i + 1) * P], col(COL_CQ), start=c == 0, stop=c == 1)
                        ins.then_inc(msq_used, 2)
                    elif kind == "kr":
                        pe.wait_ge(proj_used, N_PROJ * layer + j + 1)
                        rotate(const[64:96, C_ROTM:C_ROTM + 96], mk[64:96, 0, 0:TX])
                    elif kind == "mq":
                        pe.wait_ge(proj_used, N_PROJ * layer + j + 1)
                        rotate(const[64:96, C_ROTM:C_ROTM + 96], mq[64:96, t, 0:TX])

                def keys_norm():
                    pe.wait_ge(mdiag_ready, 2 * layer + 1)
                    pe.matmul(bank[:, BCAST, :], const[:, C_SEL0:C_SEL0 + P], diag[0], start=True, stop=False)
                    pe.matmul(bank[:, BCAST, :], const[:, C_SEL1:C_SEL1 + P], diag[1], start=False, stop=True).then_inc(mbc_ready, 1)

                def latent_norm():
                    pe.wait_ge(mdiag_ready, 2 * layer + 2)
                    pe.matmul(bank[:, BCAST, :], ones, diag[0], start=True, stop=True).then_inc(mbc_ready, 1)

                pe.wait_ge(n_ready, 8 * (r + 1))
                for j, (kind, t) in enumerate(PROJ):
                    u = PROJ_UNIT[j]
                    s = u % 2
                    if j == 0 or PROJ_UNIT[j - 1] != u:
                        pe.wait_ge(lo_done, base + u + 3)
                    if j >= 4:
                        pe.wait_ge(proj_used, N_PROJ * layer + j - 3)
                    dst = bank[:, j % 4, :]
                    w = wq if kind in ("bq", "cq", "mq", "aq") else T
                    if kind in ("bq", "bk", "ckv", "cq", "ak", "aq"):
                        second = proj_last(j)
                        for k in range(KT):
                            wh, wl = wblock(s, ((KT if second else 0) + k) * P)
                            ins = split_product(dst[:, 0:w], wh, wl, n_hi[:, k, 0:w], n_lo[:, k, 0:w], k == 0, k == KT - 1)
                    elif kind in ("vb", "va"):
                        cols, per = (P, 4) if kind == "vb" else (2 * P, 2)
                        for i in range(per):
                            tok = slice((per * t + i) * P, (per * t + i + 1) * P)
                            for k in range(KT):
                                wh, wl = wblock(s, k * cols, cols)
                                ins = split_product(dst[:, i * cols:(i + 1) * cols], n_hi[:, k, tok], n_lo[:, k, tok], wh, wl,
                                                    k == 0, k == KT - 1)
                    elif kind == "kr":
                        for k in range(KT):
                            wh, wl = wblock(s, 8 * P + k * MW, MW)
                            ins = split_product(dst[0:MW, :], wh, wl, n_hi[:, k, :], n_lo[:, k, :], k == 0, k == KT - 1)
                    elif kind == "mq":
                        if t == 0:
                            pe.wait_ge(lat_lo, 3 * layer + 2)
                        for k in range(2):
                            wh, wl = wblock(s, (k * 4 + t) * MW, MW)
                            ins = split_product(dst[0:MW, 0:w], wh, wl, h_hi[:, k, 0:w], h_lo[:, k, 0:w], k == 0, k == 1)
                    elif kind == "mk":
                        if t == 0:
                            pe.wait_ge(lat_lo, 3 * layer + 3)
                        wh, wl = wblock(s, t * P, HD)
                        ins = split_product(dst[0:HD, :], wh, wl, h_hi[:, 2, :], h_lo[:, 2, :], True, True)
                    elif kind == "vm":
                        for i in range(2):
                            tok = slice((2 * t + i) * P, (2 * t + i + 1) * P)
                            wh, wl = (x_[:, 0:512].rearrange("p (h c) -> p h c", h=4)[:, :, 64:128] for x_ in (w_hi[s], w_lo[s]))
                            ins = split_product(dst[:, i * 256:(i + 1) * 256].rearrange("p (h c) -> p h c", h=4),
                                                h_hi[:, 2, tok], h_lo[:, 2, tok], wh, wl, True, True)
                    ins.then_inc(units_done if proj_last(j) else proj_mid, 1)
                    if j:
                        after(j - 1)
                    if j == 8:
                        keys_norm()
                    if j == 9:
                        latent_norm()
                after(N_PROJ - 1)

            def attention(layer):
                todo = blocks(layer)
                b0 = block_base(layer)

                def scores(n):
                    kind, t, half, part, tile, _ = todo[n]
                    keys = slice(0, T) if part == 0 else slice(TX, T)
                    if n >= 2:
                        pe.wait_ge(exp_done, b0 + n - 1)
                    for q in range(2):
                        tok = slice((2 * part + q) * P, (2 * part + q + 1) * P)
                        rows = slice(0, MW) if kind == "m" else slice(64 * half, 64 * half + 64)
                        if kind == "a":
                            lhs, rhs = aq[rows, t, tok], ak[rows, t, keys]
                        elif kind == "b":
                            lhs, rhs = bq[rows, t, tok], bk[rows, keys]
                        else:
                            lhs, rhs = mq[rows, 2 * t + half, tok], mk[rows, 2 * t + half, keys]
                        ins = pe.matmul(bank[:, 2 * (n % 2) + q, 0:keys.stop - keys.start], lhs, rhs, start=True, stop=True)
                    ins.then_inc(s_ready, 1)

                def transposes(n):
                    part = todo[n][3]
                    pe.wait_ge(p_ready, b0 + n + 1)
                    if n:
                        pe.wait_ge(pt_a, b0 + n)
                        if x_blocks(layer, n):
                            pe.wait_ge(pt_b, sum(x_blocks(i, N_BLOCKS[i]) for i in range(layer)) + x_blocks(layer, n))
                    for k in range(4 if part == 0 else 2):
                        for q in range(2):
                            dst = bank[:, 4 + k // 2, (k % 2) * TX + q * P:(k % 2) * TX + (q + 1) * P]
                            ins = pe.transpose(dst, probs[:, n % 2, q, k * P:(k + 1) * P], ident)
                    ins.then_inc(pt_ready, 1)

                def weigh(n):
                    kind, t, half, part, tile, last = todo[n]
                    pe.wait_ge(pt_a, b0 + n + 1)
                    if part == 0:
                        pe.wait_ge(pt_b, sum(x_blocks(i, N_BLOCKS[i]) for i in range(layer)) + x_blocks(layer, n + 1))
                    if half == 0 and part == 0 and 8 * layer + tile >= 2:
                        pe.wait_ge(o_lo, 8 * layer + tile - 1)
                    vcol = {"a": (2 * t + half) * HD, "b": 256 + half * HD, "m": 384 + (2 * t + half) * HD}[kind]
                    nk = 4 if part == 0 else 2
                    for k in range(nk):
                        keytile = k if part == 0 else 2 + k
                        ins = pe.matmul(bank[64 * half:64 * half + 64, 6 + tile % 2, part * TX:(part + 1) * TX],
                                        val[:, keytile, vcol:vcol + HD],
                                        tmp[:, 2 * (n % 2) + k // 2, (k % 2) * TX:(k % 2 + 1) * TX],
                                        start=k == 0, stop=k == nk - 1)
                    if last:
                        ins.then_inc(o_ready, 1)

                pe.wait_ge(proj_used, N_PROJ * (layer + 1))
                pe.wait_ge(rot_used, N_ROT * (layer + 1))
                pe.wait_ge(kv_ready, 3 * (layer + 1))
                scores(0)
                scores(1)
                for n in range(len(todo)):
                    transposes(n)
                    if n + 2 < len(todo):
                        scores(n + 2)
                    weigh(n)

            def merge(layer):
                w = T if layer < DEPTH - 1 else TX
                base = layer * LAYER_UNITS + MERGE0
                m0 = layer * KT
                pe.wait_ge(o_lo, 8 * (layer + 1))
                with pe.Fori(0, KT) as i:
                    d = m0 + i

                    def gate(slot, at, b):
                        for k in range(KT):
                            wh, wl = wblock(slot, (at + k) * P)
                            ins = split_product(bank[:, b, 0:w], wh, wl, n_hi[:, k, 0:w], n_lo[:, k, 0:w], k == 0, k == KT - 1)
                        return ins

                    def branch(at, first, n, b):
                        pe.wait_ge(mg_used, 3 * d + b + 1)
                        for k in range(n):
                            wh, wl = wblock(1, (at + k) * P)
                            ins = split_product(bank[:, (3, 6, 7)[b], 0:w], wh, wl, h_hi[:, first + k, 0:w],
                                                h_lo[:, first + k, 0:w], k == 0, k == n - 1)
                        return ins

                    pe.wait_ge(lo_done, base + 2 * i + 3)
                    pe.wait_ge(mg_tanh, 3 * d + 1)
                    gate(0, 0, 0).then_inc(mg_ready, 1)
                    pe.wait_ge(mg_tanh, 3 * d + 2)
                    gate(0, KT, 1).then_inc(units_done, 1)
                    pe.wait_ge(lo_done, base + 2 * i + 4)
                    pe.wait_ge(mg_tanh, 3 * d + 3)
                    gate(1, 0, 2).then_inc(mg_ready, 1)
                    branch(KT, 0, 2, 0).then_inc(mg_ready, 1)
                    branch(KT + 2, 2, 4, 1).then_inc(mg_ready, 1)
                    branch(KT + 6, 6, 2, 2).then_inc(units_done, 1)

                def merged_ready(k):
                    if k == 0 or k >= KT - 2:
                        pe.wait_ge(yl_done, m0 + (k + 2 if k else KT - 1))

                down(layer * LAYER_UNITS + OUT0, visit_base(layer, 1), KT, y_hi, y_lo, w, merged_ready)

            pe.sem_inc(units_done, 2)
            pe.wait_ge(s_const, 32)
            for piece in range(EARLY_PIECES):
                reduce_ada(piece)
            norm(0, T)
            for layer in range(DEPTH):
                r = 3 * layer
                w = T if layer < DEPTH - 1 else TX
                if layer:
                    norm(r, T)
                ffn(2 * layer, r)
                norm(r + 1, T)
                project(layer, r + 1)
                attention(layer)
                merge(layer)
                norm(r + 2, w)
                ffn(2 * layer + 1, r + 2)
            norm(3 * DEPTH, TX)

        @block.vector
        def _(dve):
            steps = [0]

            def then(ins):
                steps[0] += 1
                ins.then_inc(v_step, 1)
                dve.wait_ge(v_step, steps[0])

            def rsqrt(dst, src, shape):
                v, a, b = (shape(t) for t in (rs_v, rs_a, rs_b))
                then(dve.tensor_scalar(v, src, EPS, None, ALU.add))
                then(dve.tensor_scalar(b.bitcast(I32), v.bitcast(I32), 1, None, ALU.logical_shift_right))
                then(dve.tensor_scalar(dst.bitcast(I32), b.bitcast(I32), -1.0, RSQRT_MAGIC, ALU.mult, ALU.add))
                for _ in range(4):
                    then(dve.tensor_tensor(a, dst, dst, ALU.mult))
                    then(dve.scalar_tensor_tensor(b, a, -0.5, v, ALU.mult, ALU.mult))
                    then(dve.scalar_tensor_tensor(dst, b, 1.5, dst, ALU.add, ALU.mult))

            def ada_half(piece, half):
                dve.wait_ge(ada_in[half], 16 * (piece + 1))
                for k in range(4):
                    for v in range(2):
                        c = silu_c[:, v * KT + 4 * half + k:v * KT + 4 * half + k + 1]
                        row, acc = ada_raw[half][:, k, :], ada_acc[:, v, :]
                        n = 8 * half + 2 * k + v
                        if n < 2:
                            ins = dve.tensor_scalar(acc, row, c, None, ALU.mult)
                        else:
                            dve.wait_ge(ada_step, 16 * piece + n - 1)
                            ins = dve.scalar_tensor_tensor(acc, row, c, acc, ALU.mult, ALU.add)
                        ins.then_inc(ada_step, 1)
                dve.wait_ge(ada_step, 16 * piece + 8 * half + 8)
                dve.sem_inc(ada_used, 1)

            def ada_out(piece):
                dve.wait_ge(ada_cols, piece + 1)
                for v in range(2):
                    ins = dve.tensor_tensor(mods[:, v, bass.ts(piece, 4)], bank[:, STAT, 4 * v:4 * v + 4],
                                            gains[:, bass.ds(piece * 4 + G_BADA, 4)], ALU.add)
                ins.then_inc(ada_done, 1)

            def add_square(q, w, parity):
                dve.wait_ge(sq_done, q + 1)
                dve.wait_ge(sq_added, q + 2)
                dve.tensor_tensor(sq_sum[:, 0:w], sq_sum[:, 0:w], squares[parity][:, 0:w], ALU.add).then_inc(sq_added, 1)

            def mod_col(layer, m):
                return layer * N_MOD * KT + m * KT

            def norm(r, layer, m, gain, w):
                nj = w // P
                if layer is not None:
                    at = mod_col(layer, m + 1)
                    dve.wait_ge(ada_done, layer * LP + 2 * (m + 2))
                    for v in range(2):
                        ins = dve.scalar_tensor_tensor(coef_a[:, v, :], mods[:, v, at:at + KT], 1.0, gains[:, gain:gain + KT],
                                                       ALU.add, ALU.mult)
                    then(ins)
                dve.wait_ge(stat_ready, r + 1)
                rsqrt(rstd[:, 0:nj], bank[:, STAT, 0:nj], lambda t: t[:, 0:nj])
                for j in range(nj):
                    ins = dve.tensor_scalar(diag[0][:, j * P:(j + 1) * P], ident, rstd[:, j:j + 1], None, ALU.mult)
                ins.then_inc(diag_ready, 1)
                dve.wait_ge(bcast_ready, r + 1)

                def low(dt):
                    dve.wait_ge(n_hi_done, 8 * r + dt + 1)
                    dve.tensor_tensor(n_lo[:, dt, 0:w], tmp[:, 2 + dt % 2, 0:w], n_hi[:, dt, 0:w].bitcast(F32),
                                      ALU.subtract).then_inc(n_ready, 1)

                for dt in range(KT):
                    if layer is None:
                        if dt >= 2:
                            dve.wait_ge(fin_o, dt - 1)
                        dve.tensor_tensor(tmp[:, dt % 2, 0:w], x[:, dt, 0:w], bank[:, BCAST, 0:w], ALU.mult).then_inc(fin_t, 1)
                        continue
                    dve.tensor_tensor(tmp[:, dt % 2, 0:w], x[:, dt, 0:w], bank[:, BCAST, 0:w], ALU.mult).then_inc(scaled, 1)
                    if dt:
                        low(dt - 1)
                if layer is not None:
                    low(KT - 1)

            def gate_coef(layer, m, factor):
                at = mod_col(layer, m)
                dve.wait_ge(ada_done, layer * LP + 2 * (m + 1))
                then(dve.tensor_scalar(coef_g[:, :, :], mods[:, :, at:at + KT], factor, None, ALU.mult))

            def clear_squares():
                then(dve.memset(sq_sum[:, :], 0.0))

            def down(ub, vb, yb, w, q0, extra=None):
                with dve.Fori(0, 2) as i:
                    for s in range(2):
                        if extra is not None:
                            ada_half(extra + i, s)
                        for d in range(2):
                            dt = 4 * i + 2 * s + d
                            if d == 0:
                                dve.wait_ge(y_even, yb + 2 * i + s + 1)
                            else:
                                dve.wait_ge(units_done, ub + 2 * i + s + 3)
                            for v in range(w // TX):
                                tile = tile_of(x, dt, TX, v * TX)
                                ins = dve.scalar_tensor_tensor(tile, bank[:, 4 + d, v * TX:(v + 1) * TX],
                                                               coef_g[:, v, bass.ds(dt, 1)], tile, ALU.mult, ALU.add)
                            ins.then_inc(x_done, 1)
                        if q0 is not None:
                            for d in range(2):
                                add_square(q0 + 4 * i + 2 * s + d, w, d)
                    if extra is not None:
                        ada_out(extra + i)

            def ffn(f, q0):
                w, base, layer = width(f), ffn_base(f), f // 2
                start = 0
                for g, n in enumerate(GROUPS):
                    ub = base + UP_OFF[g]
                    carries = (f, g) in ADA_UP
                    with dve.Fori(0, n // 2) as i:
                        for s in range(2):
                            tile = FT * f + start + 2 * i + s
                            if carries:
                                ada_half(ADA_UP[f, g] + i, s)
                            dve.wait_ge(tanh_done, tile + 1)
                            dve.scalar_tensor_tensor(tmp[:, 2 + s, 0:w], tmp[:, s, 0:w], 1.0, bank[:, 2 * s, 0:w],
                                                     ALU.add, ALU.mult).then_inc(silu_done, 1)
                            dve.wait_ge(silu_done, tile + 1)
                            dve.tensor_tensor(tmp[:, 4 + s, 0:w], tmp[:, 2 + s, 0:w], bank[:, 2 * s + 1, 0:w],
                                              ALU.mult).then_inc(gu_used, 1)
                            dve.wait_ge(h_hi_done, tile + 1)
                            dve.tensor_tensor(tile_of(h_lo, 2 * i + s, w), tmp[:, 4 + s, 0:w],
                                              tile_of(h_hi, 2 * i + s, w).bitcast(F32),
                                              ALU.subtract).then_inc(h_lo_done, 1)
                        if carries:
                            ada_out(ADA_UP[f, g] + i)
                    start += n
                    if g == 0:
                        gate_coef(layer, 2 + 6 * (f % 2), 0.25)
                    if g == 2:
                        clear_squares()
                    yb = (f // 2) * 28 + (f % 2) * 16 + 4 * g
                    down(base + DOWN_OFF[g], visit_base(layer, 2 * (f % 2)) + g * KT, yb, w, q0 if g == 2 else None,
                         ADA_DOWN.get((f, g)))

            def project(layer):
                wq = T if layer < DEPTH - 1 else TX
                njq = wq // P
                cosb, sinb = const[:, C_COSB:C_COSB + TX], const[:, C_SINB:C_SINB + TX]
                rots = [0]

                def rope(dst, rows, cos, sin):
                    m = N_ROT * layer + rots[0]
                    b = 4 + rots[0] % 2
                    dve.wait_ge(rot_ready, m + 1)
                    if m:
                        dve.wait_ge(rot_used, m)
                    then(dve.tensor_tensor(tmp[rows, 3, 0:TX], bank[rows, b, 0:TX], sin[rows, :], ALU.mult))
                    then(dve.tensor_tensor(dst, dst, cos[rows, :], ALU.mult))
                    dve.tensor_tensor(dst, dst, tmp[rows, 3, 0:TX], ALU.add).then_inc(rot_used, 1)
                    rots[0] += 1

                def diagonal(which, c):
                    for j in range(4):
                        ins = dve.tensor_scalar(diag[which][:, j * P:(j + 1) * P], ident, rstd[:, 4 * c + j:4 * c + j + 1],
                                                None, ALU.mult)
                    return ins

                def latent_lo(t, i, w):
                    dve.wait_ge(lat_hi, 3 * layer + i + 1)
                    src = tmp[:, (1, 2, 0)[i], 0:w]
                    dve.tensor_tensor(h_lo[:, t, 0:w], src, h_hi[:, t, 0:w].bitcast(F32), ALU.subtract).then_inc(lat_lo, 1)

                full = slice(0, P)
                for t in range(4):
                    rope(bq[:, t, 0:TX], full, cosb, sinb)
                rope(bk[:, 0:TX], full, cosb, sinb)
                dve.wait_ge(msq_used, 8 * layer + 6)
                then(dve.tensor_scalar(rs_v[:, 0:12], bank[:, STAT, 0:12], EPS, None, ALU.add))
                dve.sem_inc(mstat_used, 1)
                rsqrt_from_v(rstd[:, 0:12], lambda t: t[:, 0:12])
                diagonal(0, ST_K)
                diagonal(1, ST_K + 1).then_inc(mdiag_ready, 1)
                latent_lo(0, 0, wq)
                latent_lo(1, 1, wq)
                dve.wait_ge(mbc_ready, 2 * layer + 1)
                dve.wait_ge(rot_used, N_ROT * layer + 5)
                then(dve.tensor_tensor(bk[:, :], bk[:, :], bank[:, BCAST, :], ALU.mult))
                diagonal(0, ST_CKV).then_inc(mdiag_ready, 1)
                dve.wait_ge(mbc_ready, 2 * layer + 2)
                dve.wait_ge(proj_used, N_PROJ * layer + 6)
                dve.tensor_tensor(tmp[:, 0, :], tmp[:, 0, :], bank[:, BCAST, :], ALU.mult).then_inc(lat_f32, 1)
                latent_lo(2, 2, T)
                dve.wait_ge(msq_used, 8 * layer + 8)
                c0 = 4 * ST_CQ

                def shape(t):
                    return t[:, c0:48].rearrange("p (c j) -> p c j", j=4)[:, :, 0:njq]

                then(dve.tensor_scalar(shape(rs_v), bank[:, STAT, c0:48].rearrange("p (c j) -> p c j", j=4)[:, :, 0:njq],
                                       EPS, None, ALU.add))
                dve.sem_inc(mstat_used, 1)
                rsqrt_from_v(shape(rstd), shape)
                qs = qscale[:, :].rearrange("p (c j) -> p c j", j=4)[:, :, 0:njq]
                dve.tensor_scalar(qs[:, 0:1], shape(rstd)[:, 0:1], MLA_SCALE, None, ALU.mult)
                then(dve.tensor_scalar(qs[:, 1:9], shape(rstd)[:, 1:9], HD ** -0.5, None, ALU.mult))
                cosm, sinm = const[:, C_COSM:C_COSM + TX], const[:, C_SINM:C_SINM + TX]
                rows = slice(64, 96)
                rope(mk[rows, 0, 0:TX], rows, cosm, sinm)
                for t in range(4):
                    rope(mq[rows, t, 0:TX], rows, cosm, sinm)

            def rsqrt_from_v(dst, shape):
                v, a, b = (shape(t) for t in (rs_v, rs_a, rs_b))
                then(dve.tensor_scalar(b.bitcast(I32), v.bitcast(I32), 1, None, ALU.logical_shift_right))
                then(dve.tensor_scalar(dst.bitcast(I32), b.bitcast(I32), -1.0, RSQRT_MAGIC, ALU.mult, ALU.add))
                for _ in range(4):
                    then(dve.tensor_tensor(a, dst, dst, ALU.mult))
                    then(dve.scalar_tensor_tensor(b, a, -0.5, v, ALU.mult, ALU.mult))
                    then(dve.scalar_tensor_tensor(dst, b, 1.5, dst, ALU.add, ALU.mult))

            def attention(layer):
                todo = blocks(layer)
                b0 = block_base(layer)
                mask = const[:, C_MASK:C_MASK + TX]
                seen = [0]

                def front(n):
                    kind, t, half, part, tile, _ = todo[n]
                    keys = T if part == 0 else TX
                    p = n % 2
                    banks = bank[:, 2 * p:2 * p + 2, :]
                    if kind == "a" and part == 0:
                        h = 2 * t + half
                        bias = tmp[:, 4 + h % 2, :].rearrange("p (q k) -> p q k", q=2)
                        dve.wait_ge(bias_in[h % 2], 64 * (2 * layer + h // 2 + 1))
                        for q in range(2):
                            ins = dve.scalar_tensor_tensor(bias[:, q, :], bias[:, q, :], 1.0 / NA_SCALE, mask, ALU.mult, ALU.add)
                        then(ins)
                        dve.wait_ge(s_ready, b0 + n + 1)
                        dve.tensor_tensor(banks[:, :, 0:TX], banks[:, :, 0:TX], bias, ALU.add).then_inc(bias_used, 1)
                        dve.wait_ge(bias_used, 4 * layer + h + 1)
                    dve.wait_ge(s_ready, b0 + n + 1)
                    then(dve.tensor_reduce(mx[:, p, :], banks[:, :, 0:keys], AX.X, ALU.max))
                    if kind == "a":
                        dve.tensor_scalar(nbias[:, p, :], mx[:, p, :], -NA_SCALE, None, ALU.mult).then_inc(nb_ready, 1)
                    else:
                        c = (0 if kind == "m" else 4 * (1 + 2 * t + half)) + 2 * part
                        dve.scalar_tensor_tensor(nbias[:, p, :], mx[:, p, :], -1.0, qscale[:, c:c + 2],
                                                 ALU.mult, ALU.mult).then_inc(nb_ready, 1)

                def back(n):
                    part, p = todo[n][3], n % 2
                    keys = T if part == 0 else TX
                    dve.wait_ge(exp_done, b0 + n + 1)
                    then(dve.reciprocal(rinv[:, p, :], rsum[:, p, :]))
                    for q in range(2):
                        ins = dve.tensor_scalar(probs[:, p, q, 0:keys], probs[:, p, q, 0:keys], rinv[:, p, q:q + 1], None, ALU.mult)
                    ins.then_inc(p_ready, 1)

                def out_lo(n):
                    tile = todo[n][4]
                    w = T if layer < DEPTH - 1 else TX
                    dve.wait_ge(o_hi, 8 * layer + tile + 1)
                    dve.tensor_tensor(h_lo[:, tile, 0:w], bank[:, 6 + tile % 2, 0:w], h_hi[:, tile, 0:w].bitcast(F32),
                                      ALU.subtract).then_inc(o_lo, 1)

                front(0)
                front(1)
                back(0)
                for n in range(len(todo)):
                    if todo[n][3] == 0:
                        dve.wait_ge(pt_ready, b0 + n + 1)
                        dve.tensor_copy(tmp[:, 2 * (n % 2) + 1, :], bank[:, 5, :]).then_inc(pt_b, 1)
                    if n + 1 < len(todo):
                        back(n + 1)
                    if n and todo[n - 1][5]:
                        out_lo(n - 1)
                    if n + 2 < len(todo):
                        front(n + 2)
                out_lo(len(todo) - 1)

            def merge(layer, q0):
                w = T if layer < DEPTH - 1 else TX
                base = layer * LAYER_UNITS + MERGE0
                m0 = layer * KT
                gate_coef(layer, 5, 0.5)
                with dve.Fori(0, KT) as i:
                    d = m0 + i
                    for b in range(3):
                        if b < 2:
                            dve.wait_ge(mg_ready, 4 * d + 3 + b)
                        else:
                            dve.wait_ge(units_done, base + 2 * i + 4)
                        dve.wait_ge(mg_tanh, 3 * d + b + 4)
                        if b == 1:
                            dve.wait_ge(yl_done, d + 1)
                        dve.scalar_tensor_tensor(tmp[:, 3 + b, 0:w], tmp[:, b, 0:w], 1.0, bank[:, (3, 6, 7)[b], 0:w],
                                                 ALU.add, ALU.mult).then_inc(mg_used, 1)
                        if b == 1:
                            dve.wait_ge(mg_used, 3 * d + 5)
                            dve.tensor_tensor(tmp[:, 3, 0:w], tmp[:, 3, 0:w], tmp[:, 4, 0:w], ALU.add).then_inc(mg_add, 1)
                    dve.wait_ge(mg_used, 3 * d + 6)
                    dve.wait_ge(mg_add, d + 1)
                    dve.tensor_tensor(tmp[:, 4, 0:w], tmp[:, 3, 0:w], tmp[:, 5, 0:w], ALU.add).then_inc(mg_y, 1)
                    dve.wait_ge(yh_done, d + 1)
                    dve.tensor_tensor(tile_of(y_lo, i, w), tmp[:, 4, 0:w],
                                      tile_of(y_hi, i, w).bitcast(F32),
                                      ALU.subtract).then_inc(yl_done, 1)
                clear_squares()
                down(layer * LAYER_UNITS + OUT0, visit_base(layer, 1), layer * 28 + 12, w, q0)

            dve.sem_inc(ada_used, 2)
            dve.sem_inc(sq_added, 2)
            dve.sem_inc(gu_used, 2)
            dve.sem_inc(x_done, 2)
            dve.sem_inc(mg_used, 3)
            dve.sem_inc(yl_done, 1)
            clear_squares()
            dve.wait_ge(s_const, 32)
            dve.wait_ge(a_step, 1)
            cs = gains[:, G_C:G_C + 2 * KT]
            then(dve.scalar_tensor_tensor(rs_b[:, 0:2 * KT], rs_a[:, 0:2 * KT], 1.0, cs, ALU.add, ALU.mult))
            then(dve.tensor_scalar(silu_c[:, :], rs_b[:, 0:2 * KT], 0.5, None, ALU.mult))
            for piece in range(EARLY_PIECES):
                if piece == 1:
                    for dt in range(KT):
                        add_square(dt, T, dt % 2)
                ada_half(piece, 0)
                ada_half(piece, 1)
                ada_out(piece)
            norm(0, 0, 0, G_FFN1, T)
            for layer in range(DEPTH):
                r, g0 = 3 * layer, layer * G_LAYER
                w = T if layer < DEPTH - 1 else TX
                if layer:
                    norm(r, layer, 0, g0 + G_FFN1, T)
                ffn(2 * layer, 8 + 24 * layer)
                norm(r + 1, layer, 3, g0 + G_MIX, T)
                project(layer)
                attention(layer)
                merge(layer, 8 + 24 * layer + 8)
                norm(r + 2, layer, 6, g0 + G_FFN2, w)
                ffn(2 * layer + 1, 8 + 24 * layer + 16)
            norm(3 * DEPTH, None, 0, 0, TX)


def _constants():
    import numpy as np
    c = np.zeros((P, C_WIDTH), np.float32)
    c[:, C_ID:C_ID + P] = np.eye(P)
    c[:, C_ONES:C_ONES + P] = 1.0
    c[:, C_SEL0:C_SEL0 + HD] = 1.0
    c[:, C_SEL1 + HD:C_SEL1 + P] = 1.0

    def rotation(width):
        r = np.zeros((width, width), np.float32)
        q = width // 4
        for half in range(2):
            for i in range(q):
                a, b = half * 2 * q + i, half * 2 * q + q + i
                r[b, a] = -1.0
                r[a, b] = 1.0
        return r

    for h in range(2):
        c[h * HD:(h + 1) * HD, C_ROTB + h * HD:C_ROTB + (h + 1) * HD] = rotation(HD)
    c[HD:MW, C_ROTM + HD:C_ROTM + MW] = rotation(ROPE_M)

    cols = np.arange(GRID_W)
    c0 = np.clip(cols - 8, 0, GRID_W - 16)
    inside = (cols[None, :] >= c0[:, None]) & (cols[None, :] < c0[:, None] + 16)
    mask = np.where(inside, np.float32(0.0), np.float32(-1e30 / NA_SCALE))
    c[:, C_MASK:C_MASK + TX] = np.tile(mask, (2, 4))

    def table(width):
        half = width // 2
        freqs = np.float32(10000.0) ** (-np.arange(0, half, 2, dtype=np.float32) / np.float32(half))
        t = np.arange(TX)
        row = (t // GRID_W).astype(np.float32)[:, None] * freqs
        colm = (t % GRID_W).astype(np.float32)[:, None] * freqs
        ang = np.concatenate([row, row, colm, colm], axis=-1).astype(np.float32).T
        return np.cos(ang), np.sin(ang)

    cosb, sinb = table(HD)
    c[:, C_COSB:C_COSB + TX] = np.tile(cosb, (2, 1))
    c[:, C_SINB:C_SINB + TX] = np.tile(sinb, (2, 1))
    cosm, sinm = table(ROPE_M)
    c[HD:MW, C_COSM:C_COSM + TX] = cosm
    c[HD:MW, C_SINM:C_SINM + TX] = sinm
    c[:, C_COL + COL_MODEL] = 1.0 / D_MODEL
    c[0:HD, C_COL + COL_HEAD] = 1.0 / HD
    c[HD:P, C_COL + COL_HEAD + 1] = 1.0 / HD
    c[:, C_COL + COL_CQ] = 1.0 / 256
    c[:, C_COL + COL_CKV] = 1.0 / 128
    c[:, C_COL + COL_ONE] = 1.0
    return c


def _lay_out(a):
    import numpy as np

    def fm(v):
        return v.reshape(v.shape[:-1] + (-1, P)).swapaxes(-1, -2)

    def blocks(w, m=P):
        k, n = w.shape[-2:]
        b = w.reshape(w.shape[:-2] + (k // P, P, n // m, m))
        return np.moveaxis(b, (-4, -3, -2, -1), (-2, -3, -4, -1))

    d = {}
    both = np.concatenate([a["x"][0], a["ctx"][0]], axis=0)
    d["x_t"] = np.ascontiguousarray(both.T.reshape(KT, P, T).transpose(1, 0, 2))
    gates = np.stack([a["ffn1_w_gate"], a["ffn2_w_gate"]], 1).reshape(2 * DEPTH, D_MODEL, D_FF)
    ups = np.stack([a["ffn1_w_up"], a["ffn2_w_up"]], 1).reshape(2 * DEPTH, D_MODEL, D_FF)
    up = np.stack([blocks(gates), blocks(ups)], 3)
    d["w_up"] = np.ascontiguousarray(up.reshape(2 * DEPTH, FT, P, UNIT))
    downs = np.stack([a["ffn1_w_down"], a["ffn2_w_down"]], 1).reshape(2 * DEPTH, D_FF, D_MODEL)
    db = blocks(downs)
    db = db.reshape(2 * DEPTH, KT // 2, 2, P, FT, P).transpose(0, 1, 3, 2, 4, 5)
    first = np.stack([db[..., 0:8, :], db[..., 8:16, :]], 1)
    d["w_down"] = np.ascontiguousarray(first.reshape(2 * DEPTH, 2, KT // 2, P, UNIT))
    d["w_down_last"] = np.ascontiguousarray(db[..., 16:22, :].reshape(2 * DEPTH, KT // 2, P, 12 * P))
    ada = a["w_ada"].reshape(DEPTH, 2, 4, P, LP, 512).transpose(0, 4, 1, 3, 2, 5)
    d["w_ada"] = np.ascontiguousarray(ada.reshape(PIECES, 2, P, 4, 512))

    w_in = a["w_in"]
    q_order = np.concatenate([np.arange(64) + 64 * h for t in range(4) for h in (t, 4 + t)])
    s = np.cumsum([0, 256, 256, 256, 512, 128, 128, 256, 128, 32, 3072])
    part = {n: w_in[:, :, s[i]:s[i + 1]] for i, n in enumerate(("aq", "ak", "av", "bq", "bk", "bv", "cq", "ckv", "kr", "gate"))}
    part["bq"] = part["bq"][:, :, q_order]

    def rows(w):
        return w.reshape(DEPTH, -1, P, w.shape[-1]).transpose(0, 2, 1, 3).reshape(DEPTH, P, -1)

    def pair(w):
        return blocks(w).transpose(0, 2, 1, 3, 4).reshape(DEPTH, P, -1)

    kr = np.concatenate([np.zeros((DEPTH, D_MODEL, HD), np.float32), part["kr"]], -1)
    mix = [pair(part["bq"][:, :, 0:256]), pair(part["bq"][:, :, 256:512]),
           pair(np.concatenate([part["bk"], part["ckv"]], -1)), pair(part["cq"]),
           rows(part["bv"]), rows(kr), rows(a["mla_w_uq"]), rows(a["mla_w_ukv"]),
           pair(part["ak"]), pair(part["aq"]), rows(part["av"])]
    d["w_mix"] = np.ascontiguousarray(np.concatenate(mix, -1))
    gate = blocks(part["gate"]).reshape(DEPTH, 3, KT, P, KT, P)
    wb = a["w_branch_b"][:, q_order, :]
    br = np.concatenate([blocks(a["w_branch_a"]), blocks(wb), blocks(a["w_branch_c"])], 3)
    u0 = np.stack([gate[:, 0], gate[:, 1]], 3)
    u1 = np.stack([gate[:, 2], br], 3)
    d["w_merge"] = np.ascontiguousarray(np.stack([u0, u1], 2).reshape(DEPTH, 2 * KT, P, UNIT))
    wo = blocks(a["w_out"]).reshape(DEPTH, KT // 2, 2, P, KT, P).transpose(0, 1, 3, 2, 4, 5)
    d["w_out"] = np.ascontiguousarray(wo.reshape(DEPTH, KT // 2, P, UNIT))
    d["rel_bias"] = np.tile(a["na_rel_bias"], GRID_W)

    cols = []
    for i in range(DEPTH):
        cols += [fm(a["ffn1_norm"][i]), fm(a["mix_norm"][i]), fm(a["ffn2_norm"][i]), fm(a["mla_q_norm"][i]),
                 fm(a["mla_kv_norm"][i]), np.tile(a["gqa_q_norm"][i], 2)[:, None], np.tile(a["gqa_k_norm"][i], 2)[:, None]]
    cols += [fm(a["final_norm"]), fm(a["c"][0]), fm(a["c_ctx"])]
    cols += [fm(a["b_ada"][i]) for i in range(DEPTH)]
    d["gains"] = np.ascontiguousarray(np.concatenate(cols, 1))
    d["const"] = _constants()
    return d


def kernel(**inputs):
    import numpy as np
    import concourse.bacc as bacc
    from concourse.bass_utils import run_bass_kernel_spmd

    arrays = _lay_out({k: np.asarray(v) for k, v in inputs.items()})
    nc = bacc.Bacc("TRN2", target_bir_lowering=False, num_devices=1)
    dram = {n: nc.dram_tensor(n, v.shape, mybir.dt.from_np(v.dtype), kind="ExternalInput").ap() for n, v in arrays.items()}
    out = nc.dram_tensor("out_t", (P, KT, TX), F32, kind="ExternalOutput").ap()
    build(nc, dram, out)
    r = run_bass_kernel_spmd(nc, [arrays], core_ids=[0])
    got = r.results[0]["out_t"]
    return np.ascontiguousarray(got.transpose(2, 1, 0).reshape(1, TX, D_MODEL))
```

```python
from contextlib import ExitStack

import concourse.bass as bass
from concourse import mybir

F32 = mybir.dt.float32
F32R = mybir.dt.float32r
I32 = mybir.dt.int32
ACT = mybir.ActivationFunctionType
ALU = mybir.AluOpType
AX = mybir.AxisListType

P = 128
D_MODEL = 1024
DEPTH = 2
TX = 256
T = 512
KT = D_MODEL // P
D_FF = ((8 * D_MODEL // 3 + 127) // 128) * 128
FT = D_FF // P
GROUPS = (8, 8, 6)
GRID_W = 64
N_MOD = 9
EPS = 1e-6
HD = 64
ROPE_M = 32
MW = HD + ROPE_M
NA_SCALE = HD ** -0.5
MLA_SCALE = MW ** -0.5
RSQRT_MAGIC = 1597463007.0
NA_DR, NA_DC = 15, 31
UNIT = 16 * P

UP_OFF = (0, 12, 24)
DOWN_OFF = (8, 20, 30)
FFN_UNITS = 34
MIX_SIZES = (2048, 2048, 2048, 2048, 8 * P + 8 * MW, 2 * 4 * MW, 512, 2048, 2048, 2048)
MIX_UNITS = len(MIX_SIZES)
MERGE_UNITS = 2 * KT
OUT_UNITS = KT // 2
MIX0 = FFN_UNITS
MERGE0 = MIX0 + MIX_UNITS
OUT0 = MERGE0 + MERGE_UNITS
FFN2_0 = OUT0 + OUT_UNITS
LAYER_UNITS = FFN2_0 + FFN_UNITS
TOTAL_UNITS = DEPTH * LAYER_UNITS
SHARED0 = (DEPTH - 1) * LAYER_UNITS + MERGE0
OWN = 10 * P
VISITS = (3 * KT, KT, 3 * KT)
LAYER_VISITS = sum(VISITS)

PIECES = DEPTH * N_MOD * D_MODEL // 512
LP = PIECES // DEPTH
EARLY_PIECES = 4
ADA_UP = {(0, 0): 4, (0, 1): 10, (0, 2): 16, (1, 1): 19, (1, 2): 25, (2, 0): 28, (2, 1): 32}
ADA_DOWN = {(0, 0): 8, (0, 1): 14, (1, 1): 23}


G_FFN1, G_MIX, G_FFN2, G_CQ, G_CKV, G_Q, G_K = 0, 8, 16, 24, 26, 27, 28
G_LAYER = 29
G_FINAL = DEPTH * G_LAYER
G_BADA = G_FINAL + KT
G_WIDTH = G_BADA + DEPTH * N_MOD * KT
C_ID, C_ONES, C_SEL0, C_SEL1, C_ROTB, C_ROTM, C_MASK, C_COSB, C_SINB, C_COSM, C_SINM, C_COL = (
    0, 128, 256, 384, 512, 640, 768, 1024, 1280, 1536, 1792, 2048)
C_WIDTH = C_COL + 6
COL_MODEL, COL_HEAD, COL_CQ, COL_CKV, COL_ONE = 0, 1, 3, 4, 5

ST_K, ST_CKV, ST_CQ, ST_Q = 0, 2, 3, 4


def build(nc, dram, out):
    ctx = ExitStack()
    with ctx:
        def sb(name, shape, dt=F32, scope=ctx):
            return scope.enter_context(nc.sbuf_tensor(name, shape, dt))

        def sem(name):
            return ctx.enter_context(nc.semaphore(name))

        x = sb("x", [P, KT, T])
        n_hi = sb("n_hi", [P, KT, T], F32R)
        n_lo = sb("n_lo", [P, KT, T], F32R)
        h_hi = sb("h_hi", [P, 8, T], F32R)
        w_raw = [sb(f"w_raw{s}", [P, UNIT]) for s in range(2)]
        w_hi = [sb(f"w_hi{s}", [P, UNIT], F32R) for s in range(2)]
        w_lo = [sb(f"w_lo{s}", [P, UNIT], F32R) for s in range(2)]
        tmp = sb("tmp", [P, 6, T])
        probs = sb("probs", [P, 2, 2, T])
        const = sb("const_sb", [P, C_WIDTH])
        gains = sb("gains_sb", [P, G_WIDTH])
        mods = sb("mods", [P, 2, DEPTH * N_MOD * KT])
        coef_a = sb("coef_a", [P, 2, KT])
        coef_g = sb("coef_g", [P, 2, KT])
        rstd = sb("rstd", [P, 48])
        rs_v = sb("rs_v", [P, 48])
        rs_a = sb("rs_a", [P, 48])
        rs_b = sb("rs_b", [P, 48])
        qscale = sb("qscale", [P, 36])
        mx = sb("mx", [P, 2, 2])
        nbias = sb("nbias", [P, 2, 2])
        rsum = sb("rsum", [P, 2, 2])
        rinv = sb("rinv", [P, 2, 2])
        with ExitStack() as outer:
            h_lo = sb("h_lo", [P, 8, T], F32R, outer)
            with ExitStack() as s:
                bq = sb("bq", [P, 4, T], F32, s)
                bk = sb("bk", [P, 2, T], F32, s)
                aq = sb("aq", [P, 2, T], F32, s)
                ak = sb("ak", [P, 2, T], F32, s)
                mq = sb("mq", [P, 4, T], F32, s)
                mk = sb("mk", [P, 4, T], F32, s)
                val = sb("val", [P, 4, 640], F32, s)
            with ExitStack() as s:
                sq_sum = sb("sq_sum", [P, T], F32, s)
                y_hi = sb("y_hi", [P, KT, T], F32R, s)
                y_lo = sb("y_lo", [P, KT, T], F32R, s)
            with ExitStack() as s:
                sb("below_ada", [P, T], F32, s)
                silu_b = sb("silu_b", [P, 2, D_MODEL], F32, s)
                ada_raw = [sb(f"ada_raw{i}", [P, 2, D_MODEL], F32, s) for i in range(2)]
                ada_junk = sb("ada_junk", [P, 2, D_MODEL], F32, s)
                ada_help = sb("ada_help", [P, D_MODEL], F32, s)
            with ExitStack() as s:
                sb("below_staged", [P, T], F32, s)
                staged = sb("staged", [P, KT, TX], F32, s)
        with ExitStack() as s:
            sb("below_ak_odd", [P, 6, T], F32, s)
            ak_odd = sb("ak_odd", [P, 2, T], F32, s)

        bank = ctx.enter_context(nc.psum_tensor("bank", [P, 8, 512], F32))
        STAT, BCAST = 6, 7

        squares = [probs[:, 1, i, :] for i in range(2)]
        diag = [probs[:, 0, i, :] for i in range(2)]
        ident = const[:, C_ID:C_ID + P]
        ones = const[:, C_ONES:C_ONES + P]

        def col(i, n=1):
            return const[:, C_COL + i:C_COL + i + n]

        s_const = sem("s_const")
        s_x = sem("s_x")
        raw_in = [sem(f"raw_in{i}") for i in range(2)]
        hi_done = sem("hi_done")
        lo_done = sem("lo_done")
        units_done = sem("units_done")
        hi_rest = sem("hi_rest")
        lo_rest = sem("lo_rest")
        ada_in = [sem(f"ada_in{i}") for i in range(2)]
        ada_used = sem("ada_used")
        ada_step = sem("ada_step")
        cond_in = sem("cond_in")
        cond_tanh = sem("cond_tanh")
        silu_ready = sem("silu_ready")
        help_product = sem("help_product")
        help_sum = sem("help_sum")
        ada_done = sem("ada_done")
        sq_done = sem("sq_done")
        sq_added = sem("sq_added")
        stat_ready = sem("stat_ready")
        diag_ready = sem("diag_ready")
        bcast_ready = sem("bcast_ready")
        scaled = sem("scaled")
        modulated = sem("modulated")
        n_hi_done = sem("n_hi_done")
        n_ready = sem("n_ready")
        tanh_done = sem("tanh_done")
        silu_done = sem("silu_done")
        gu_used = sem("gu_used")
        h_hi_done = sem("h_hi_done")
        h_lo_done = sem("h_lo_done")
        y_even = sem("y_even")
        x_done = sem("x_done")
        proj_mid = sem("proj_mid")
        proj_used = sem("proj_used")
        msq_ready = sem("msq_ready")
        msq_used = sem("msq_used")
        rot_ready = sem("rot_ready")
        rot_used = sem("rot_used")
        mstat_used = sem("mstat_used")
        mdiag_ready = sem("mdiag_ready")
        mbc_ready = sem("mbc_ready")
        lat_f32 = sem("lat_f32")
        lat_hi = sem("lat_hi")
        lat_lo = sem("lat_lo")
        kv_ready = sem("kv_ready")
        zeroed = sem("zeroed")
        bias_in = [sem(f"bias_in{i}") for i in range(2)]
        bias_used = sem("bias_used")
        s_ready = sem("s_ready")
        nb_ready = sem("nb_ready")
        exp_done = sem("exp_done")
        p_ready = sem("p_ready")
        pt_ready = sem("pt_ready")
        pt_a = sem("pt_a")
        pt_b = sem("pt_b")
        o_ready = sem("o_ready")
        o_hi = sem("o_hi")
        o_lo = sem("o_lo")
        mg_ready = sem("mg_ready")
        mg_tanh = sem("mg_tanh")
        mg_used = sem("mg_used")
        mg_add = sem("mg_add")
        mg_y = sem("mg_y")
        yh_done = sem("yh_done")
        yl_done = sem("yl_done")
        v_step = sem("v_step")
        fin_t = sem("fin_t")
        fin_o = sem("fin_o")
        s_out = sem("s_out")

        def ffn_base(f):
            return (f // 2) * LAYER_UNITS + (f % 2) * FFN2_0

        def visit_base(layer, phase):
            return layer * LAYER_VISITS + sum(VISITS[:phase])

        def width(f):
            return TX if f == 2 * DEPTH - 1 else T

        def tile_of(t, i, w=T, at=0):
            return t[:, bass.ds(i, 1), at:at + w].rearrange("p a b -> p (a b)")

        def blocks(layer):
            parts = (0, 1) if layer < DEPTH - 1 else (0,)
            found = []
            for tile in range(8):
                for half in range(2):
                    for part in parts:
                        kind, t = ("a", tile) if tile < 2 else ("b", tile - 2) if tile < 6 else ("m", tile - 6)
                        found.append((kind, t, half, part, tile, half == 1 and part == parts[-1]))
            return found

        N_BLOCKS = [len(blocks(i)) for i in range(DEPTH)]

        def block_base(layer):
            return sum(N_BLOCKS[:layer])

        def x_blocks(layer, n):
            return sum(b[3] == 0 for b in blocks(layer)[:n])

        PROJ = [("bq", 0), ("bq", 1), ("bq", 2), ("bq", 3), ("bk", 0), ("ckv", 0), ("cq", 0), ("cq", 1),
                ("vb", 0), ("kr", 0), ("mq", 0), ("mq", 1), ("mq", 2), ("mq", 3),
                ("mk", 0), ("mk", 1), ("mk", 2), ("mk", 3), ("vm", 0), ("vm", 1),
                ("ak", 0), ("ak", 1), ("aq", 0), ("aq", 1), ("va", 0), ("va", 1)]
        PROJ_UNIT = [0, 0, 1, 1, 2, 2, 3, 3, 4, 4, 5, 5, 5, 5, 6, 6, 6, 6, 6, 6, 7, 7, 8, 8, 9, 9]
        N_PROJ = len(PROJ)

        def proj_last(j):
            return j + 1 == N_PROJ or PROJ_UNIT[j + 1] != PROJ_UNIT[j]

        def wait_proj(e, layer, j):
            if proj_last(j):
                e.wait_ge(units_done, layer * LAYER_UNITS + MIX0 + PROJ_UNIT[j] + 3)
            else:
                mids = sum(not proj_last(i) for i in range(N_PROJ))
                e.wait_ge(proj_mid, layer * mids + sum(not proj_last(i) for i in range(j + 1)))

        ROT = [("bq", 0), ("bq", 1), ("bq", 2), ("bq", 3), ("bk", 0), ("kr", 0),
               ("mq", 0), ("mq", 1), ("mq", 2), ("mq", 3)]
        N_ROT = len(ROT)

        def load_bias(queue, layer, h):
            for qr in range(4):
                src = bass.AP(dram["rel_bias"].tensor, ((layer * 4 + h) * NA_DR + 7 - qr) * GRID_W * NA_DC + 15,
                              [[NA_DC - 1, GRID_W], [GRID_W * NA_DC, 4], [1, GRID_W]])
                dst = tmp[64 * (qr % 2):64 * (qr % 2) + 64, 4 + h % 2, (qr // 2) * 256:(qr // 2) * 256 + 256]
                queue.dma_start(dst.rearrange("p (a b) -> p a b", a=4), src).then_inc(bias_in[h % 2], 16)

        block = ctx.enter_context(nc.Block())

        @block.sync
        def _(sp):
            def load(unit, slot, src, size=UNIT, shared=False):
                count = unit + 1
                sp.wait_ge(lo_done, count)
                if shared:
                    sp.wait_ge(lo_rest, count)
                sp.dma_start(w_raw[slot][:, 0:size], src).then_inc(raw_in[slot], 16)

            def load_ada(piece):
                for half in range(2):
                    sp.wait_ge(ada_used, 2 * piece + half + 1)
                    sp.dma_start(ada_raw[half][:, :, :], dram["w_ada"][piece, half]).then_inc(ada_in[half], 16)

            def load_conditions():
                for v in range(2):
                    sp.dma_start(silu_b[:, v, :], dram["cond"][v:v + 1, :].broadcast_to([P, D_MODEL])).then_inc(cond_in, 16)

            def load_ffn(f):
                base = ffn_base(f)
                start = 0
                for g, n in enumerate(GROUPS):
                    with sp.Fori(0, n // 2) as i:
                        for s in range(2):
                            load(base + UP_OFF[g] + 2 * i + s, s, dram["w_up"][f, start + 2 * i + s],
                                 shared=f == 2 * DEPTH - 1)
                        if (f, g) in ADA_UP:
                            load_ada(ADA_UP[f, g] + i)
                    if f == 1 and g == 0:
                        sp.wait_ge(units_done, base + 2)
                        load_conditions()
                    src = dram["w_down"] if n == 8 else dram["w_down_last"]
                    with sp.Fori(0, 2) as i:
                        for s in range(2):
                            at = src[f, g, 2 * i + s] if n == 8 else src[f, 2 * i + s]
                            load(base + DOWN_OFF[g] + 2 * i + s, s, at, 2 * n * P, f == 2 * DEPTH - 1)
                        if (f, g) in ADA_DOWN:
                            load_ada(ADA_DOWN[f, g] + i)
                    start += n

            load_conditions()
            sp.dma_start(gains[:, :], dram["gains"]).then_inc(s_const, 16)
            sp.dma_start(const[:, :], dram["const"]).then_inc(s_const, 16)
            load_ada(0)
            sp.dma_start(x[:, :, :], dram["x_t"]).then_inc(s_x, 16)
            for piece in range(1, EARLY_PIECES):
                load_ada(piece)
            for layer in range(DEPTH):
                load_ffn(2 * layer)
                base = layer * LAYER_UNITS
                at = 0
                for u, size in enumerate(MIX_SIZES):
                    load(base + MIX0 + u, u % 2, dram["w_mix"][layer, :, at:at + size], size)
                    at += size
                for h in range(2):
                    load_bias(sp, layer, h)
                with sp.Fori(0, KT) as i:
                    for s in range(2):
                        load(base + MERGE0 + 2 * i + s, s, dram["w_merge"][layer, 2 * i + s], shared=layer == DEPTH - 1)
                with sp.Fori(0, OUT_UNITS // 2) as i:
                    for s in range(2):
                        load(base + OUT0 + 2 * i + s, s, dram["w_out"][layer, 2 * i + s], shared=layer == DEPTH - 1)
                load_ffn(2 * layer + 1)
            for part in range(2):
                sp.wait_ge(fin_o, 4 * (part + 1))
                sp.dma_start(out[:, 4 * part:4 * part + 4, :], staged[:, 4 * part:4 * part + 4, :]).then_inc(s_out, 16)
            sp.wait_ge(s_out, 32)

        @block.gpsimd
        def _(pool):
            pool.sem_inc(lo_done, 2)
            pool.wait_ge(silu_ready, 1)
            for piece in range(EARLY_PIECES):
                for half in range(2):
                    pool.wait_ge(ada_in[half], 16 * (piece + 1))
                    if piece or half:
                        pool.wait_ge(help_sum, 2 * piece + half)
                    pool.tensor_tensor(ada_help[:, :], ada_raw[half][:, 1, :], silu_b[:, 1, :], ALU.mult).then_inc(help_product, 1)
            for start, end, cols in ((0, SHARED0, UNIT), (SHARED0, TOTAL_UNITS, OWN)):
                with pool.Fori(start // 2, end // 2) as i:
                    for s in range(2):
                        pool.wait_ge(hi_done, 2 * i + s + 1)
                        pool.tensor_tensor(w_lo[s][:, 0:cols], w_raw[s][:, 0:cols], w_hi[s][:, 0:cols].bitcast(F32),
                                           ALU.subtract).then_inc(lo_done, 1)

        @block.scalar
        def _(act):
            def split_hi(unit, slot, turn, shared=False):
                act.wait_ge(units_done, unit + 1)
                act.wait_ge(raw_in[slot], 16 * (turn + 1))
                if not shared:
                    act.activation(w_hi[slot][:, :], w_raw[slot][:, :], ACT.Copy).then_inc(hi_done, 1)
                else:
                    act.activation(w_hi[slot][:, 0:OWN], w_raw[slot][:, 0:OWN], ACT.Copy).then_inc(hi_done, 1)
                    act.activation(w_hi[slot][:, OWN:], w_raw[slot][:, OWN:], ACT.Copy).then_inc(hi_rest, 1)

            def next_hi(base, i, s, shared=False):
                split_hi(base + 2 * i + s + 2, s, base // 2 + i + 1, shared)

            def square(visit, q, dt, w, parity):
                act.wait_ge(x_done, visit + 3)
                act.wait_ge(sq_added, q + 1)
                act.activation(squares[parity][:, 0:w], tile_of(x, dt, w), ACT.Square).then_inc(sq_done, 1)

            def norm(r, layer, m, w):
                for dt in range(KT):
                    at = layer * N_MOD * KT + m * KT + dt
                    act.wait_ge(scaled, 8 * r + dt + 1)
                    if 8 * r + dt >= 2:
                        act.wait_ge(n_ready, 8 * r + dt - 1)
                    for v in range(w // TX):
                        ins = act.activation(tmp[:, 2 + dt % 2, v * TX:(v + 1) * TX], tmp[:, dt % 2, v * TX:(v + 1) * TX],
                                             ACT.Identity, scale=coef_a[:, v, dt:dt + 1], bias=mods[:, v, at:at + 1])
                    ins.then_inc(modulated, 1)
                    act.wait_ge(modulated, 8 * r + dt + 1)
                    act.activation(n_hi[:, dt, 0:w], tmp[:, 2 + dt % 2, 0:w], ACT.Copy).then_inc(n_hi_done, 1)

            def tanh_conditions(f):
                act.wait_ge(cond_in, 32 * (f + 1))
                act.activation(ada_junk[:, :, :], silu_b[:, :, :], ACT.Tanh, scale=0.5).then_inc(cond_tanh, 1)

            def ffn(f, q0):
                w, base, layer = width(f), ffn_base(f), f // 2
                start = 0
                for g, n in enumerate(GROUPS):
                    if f == 1 and g == 1:
                        tanh_conditions(f)
                    ub, db = base + UP_OFF[g], base + DOWN_OFF[g]
                    vb = visit_base(layer, 2 * (f % 2)) + g * KT
                    last = f == 2 * DEPTH - 1 and g == 2
                    with act.Fori(0, n // 2) as i:
                        for s in range(2):
                            tile = FT * f + start + 2 * i + s
                            act.wait_ge(units_done, ub + 2 * i + s + 3)
                            act.activation(tmp[:, s, 0:w], bank[:, 2 * s, 0:w], ACT.Tanh, scale=0.5).then_inc(tanh_done, 1)
                            next_hi(ub, i, s, f == 2 * DEPTH - 1)
                            act.wait_ge(gu_used, tile + 3)
                            act.activation(tile_of(h_hi, 2 * i + s, w), tmp[:, 4 + s, 0:w], ACT.Copy).then_inc(h_hi_done, 1)
                    if g < 2:
                        with act.Fori(0, 2) as i:
                            for s in range(2):
                                next_hi(db, i, s, f == 2 * DEPTH - 1)
                    elif not last:
                        with act.Fori(0, 2) as i:
                            for s in range(2):
                                for d in range(2):
                                    square(vb + 4 * i + 2 * s + d, q0 + 4 * i + 2 * s + d, 4 * i + 2 * s + d, w, d)
                                next_hi(db, i, s, f == 2 * DEPTH - 1)
                    else:
                        for i in range(2):
                            for s in range(2):
                                if i == 0:
                                    next_hi(db, i, s, f == 2 * DEPTH - 1)
                                for d in range(2):
                                    square(vb + 4 * i + 2 * s + d, q0 + 4 * i + 2 * s + d, 4 * i + 2 * s + d, w, d)
                    start += n

            def project(layer):
                wq = T if layer < DEPTH - 1 else TX
                base = layer * LAYER_UNITS + MIX0
                g0 = layer * G_LAYER
                n_sq = 0
                for j, (kind, t) in enumerate(PROJ):
                    src = bank[:, j % 4, :]
                    wait_proj(act, layer, j)
                    u = PROJ_UNIT[j]
                    if proj_last(j) and j < N_PROJ - 1:
                        next_hi(base + u - u % 2, 0, u % 2, layer == DEPTH - 1 and u >= MIX_UNITS - 2)
                    w = wq if kind in ("bq", "cq", "mq", "aq") else T
                    if kind in ("bq", "bk", "ckv", "cq"):
                        k = 8 * layer + n_sq
                        if k >= 2:
                            act.wait_ge(msq_used, k - 1)
                        act.activation(squares[n_sq % 2][:, 0:w], src[:, 0:w], ACT.Square).then_inc(msq_ready, 1)
                        n_sq += 1
                    if kind == "bq":
                        act.activation(bq[:, t, 0:w], src[:, 0:w], ACT.Copy,
                                       scale=gains[:, g0 + G_Q:g0 + G_Q + 1]).then_inc(proj_used, 1)
                    elif kind == "bk":
                        act.activation(bk[:, 0, :], src, ACT.Copy, scale=gains[:, g0 + G_K:g0 + G_K + 1]).then_inc(proj_used, 1)
                    elif kind == "ckv":
                        act.activation(tmp[:, 0, :], src, ACT.Copy, scale=gains[:, g0 + G_CKV:g0 + G_CKV + 1]).then_inc(proj_used, 1)
                    elif kind == "cq":
                        g = g0 + G_CQ + t
                        act.activation(tmp[:, 1 + t, 0:w], src[:, 0:w], ACT.Copy, scale=gains[:, g:g + 1]).then_inc(proj_used, 1)
                        act.wait_ge(proj_used, N_PROJ * layer + j + 1)
                        act.activation(h_hi[:, t, 0:w], tmp[:, 1 + t, 0:w], ACT.Copy).then_inc(lat_hi, 1)
                    elif kind == "vb":
                        act.activation(val[:, :, 256:384], src.rearrange("p (j c) -> p j c", j=4), ACT.Copy).then_inc(proj_used, 1)
                    elif kind == "vm":
                        act.activation(val[:, 2 * t:2 * t + 2, 384:640], src.rearrange("p (j c) -> p j c", j=2),
                                       ACT.Copy).then_inc(proj_used, 1)
                    elif kind == "va":
                        act.activation(val[:, 2 * t:2 * t + 2, 0:256], src.rearrange("p (j c) -> p j c", j=2),
                                       ACT.Copy).then_inc(proj_used, 1)
                    elif kind == "kr":
                        act.activation(mk[64:96, 0, :], src[64:96, :], ACT.Copy).then_inc(proj_used, 1)
                        act.wait_ge(lat_f32, layer + 1)
                        act.activation(h_hi[:, 2, :], tmp[:, 0, :], ACT.Copy).then_inc(lat_hi, 1)
                    elif kind == "mk":
                        act.activation(mk[0:64, t, :], src[0:64, :], ACT.Copy).then_inc(proj_used, 1)
                    elif kind == "ak":
                        act.wait_ge(zeroed, layer + 1)
                        act.activation(ak[0:64, t, :], src[0:64, :], ACT.Copy)
                        act.activation(ak_odd[64:128, t, :], src[64:128, :], ACT.Copy).then_inc(proj_used, 1)
                    else:
                        rows = 96 if kind == "mq" else 128
                        dst = {"mq": mq, "aq": aq}[kind]
                        act.activation(dst[0:rows, t, 0:w], src[0:rows, 0:w], ACT.Copy).then_inc(proj_used, 1)
                    if (kind, t) == ("ak", 1):
                        act.wait_ge(rot_used, N_ROT * layer + 6)
                        for head in range(1, 4):
                            act.activation(mk[64:96, head, :], mk[64:96, 0, :], ACT.Copy).then_inc(kv_ready, 1)
                next_hi(base + u - u % 2, 0, u % 2, layer == DEPTH - 1)

            def attention(layer):
                todo = blocks(layer)
                b0 = block_base(layer)

                def exps(n):
                    kind, t, half, part, tile, _ = todo[n]
                    keys = T if part == 0 else TX
                    act.wait_ge(nb_ready, b0 + n + 1)
                    for q in range(2):
                        j = 2 * part + q
                        c = {"b": 4 * (1 + 2 * t + half), "m": 0, "a": 0}[kind] + j
                        scale = NA_SCALE if kind == "a" else qscale[:, c:c + 1]
                        ins = act.activation(probs[:, n % 2, q, 0:keys], bank[:, 2 * (n % 2) + q, 0:keys], ACT.Exp,
                                             bias=nbias[:, n % 2, q:q + 1], scale=scale,
                                             accum_out=rsum[:, n % 2, q:q + 1])
                    ins.then_inc(exp_done, 1)
                    if kind == "a" and part == 0 and tile == 0:
                        h = half + 2
                        act.wait_ge(bias_used, 4 * layer + half + 1)
                        load_bias(act, layer, h)

                def out_hi(n):
                    tile = todo[n][4]
                    w = T if layer < DEPTH - 1 else TX
                    act.wait_ge(o_ready, 8 * layer + tile + 1)
                    act.activation(h_hi[:, tile, 0:w], bank[:, 6 + tile % 2, 0:w], ACT.Copy).then_inc(o_hi, 1)

                exps(0)
                for n in range(len(todo)):
                    if n + 1 < len(todo):
                        exps(n + 1)
                    act.wait_ge(pt_ready, b0 + n + 1)
                    act.activation(tmp[:, 2 * (n % 2), :], bank[:, 4, :], ACT.Copy).then_inc(pt_a, 1)
                    if n >= 2 and todo[n - 2][5]:
                        out_hi(n - 2)
                out_hi(len(todo) - 1)

            def merge(layer):
                w = T if layer < DEPTH - 1 else TX
                base = layer * LAYER_UNITS + MERGE0
                m0 = layer * KT
                with act.Fori(0, KT) as i:
                    d = m0 + i
                    act.wait_ge(mg_used, 3 * d + 3)
                    act.wait_ge(mg_ready, 4 * d + 1)
                    act.activation(tmp[:, 0, 0:w], bank[:, 0, 0:w], ACT.Tanh, scale=0.5).then_inc(mg_tanh, 1)
                    next_hi(base, i, 0, layer == DEPTH - 1)
                    act.activation(tmp[:, 1, 0:w], bank[:, 1, 0:w], ACT.Tanh, scale=0.5).then_inc(mg_tanh, 1)
                    act.wait_ge(mg_ready, 4 * d + 2)
                    act.activation(tmp[:, 2, 0:w], bank[:, 2, 0:w], ACT.Tanh, scale=0.5).then_inc(mg_tanh, 1)
                    next_hi(base, i, 1, layer == DEPTH - 1)
                    act.wait_ge(mg_y, d + 1)
                    act.activation(tile_of(y_hi, i, w), tmp[:, 4, 0:w], ACT.Copy).then_inc(yh_done, 1)
                base = layer * LAYER_UNITS + OUT0
                vb = visit_base(layer, 1)
                q0 = 8 + 24 * layer + 8
                with act.Fori(0, OUT_UNITS // 2) as i:
                    for s in range(2):
                        for d in range(2):
                            square(vb + 4 * i + 2 * s + d, q0 + 4 * i + 2 * s + d, 4 * i + 2 * s + d, w, d)
                        next_hi(base, i, s, layer == DEPTH - 1)

            act.sem_inc(mg_tanh, 3)
            tanh_conditions(0)
            act.wait_ge(s_const, 32)

            def help_sums(piece):
                for half in range(2):
                    at = 4 * piece + 2 * half + 1
                    act.wait_ge(help_product, 2 * piece + half + 1)
                    act.activation(ada_help[:, :], ada_help[:, :], ACT.Copy, accum_out=mods[:, 1, at:at + 1]).then_inc(help_sum, 1)

            help_sums(0)
            for dt in range(KT):
                if dt == 0:
                    act.wait_ge(s_x, 16)
                act.wait_ge(sq_added, dt + 1)
                act.activation(squares[dt % 2], x[:, dt, :], ACT.Square).then_inc(sq_done, 1)
            for piece in range(1, EARLY_PIECES):
                help_sums(piece)
            for s in range(2):
                split_hi(s, s, 0)
            for layer in range(DEPTH):
                r = 3 * layer
                w = T if layer < DEPTH - 1 else TX
                norm(r, layer, 0, T)
                ffn(2 * layer, 8 + 24 * layer)
                norm(r + 1, layer, 3, T)
                project(layer)
                attention(layer)
                merge(layer)
                norm(r + 2, layer, 6, w)
                ffn(2 * layer + 1, 8 + 24 * layer + 16)
            for dt in range(KT):
                act.wait_ge(fin_t, dt + 1)
                act.activation(staged[:, dt, :], tmp[:, dt % 2, 0:TX], ACT.Copy,
                               scale=gains[:, G_FINAL + dt:G_FINAL + dt + 1]).then_inc(fin_o, 1)

        @block.tensor
        def _(pe):
            def split_product(dst, wh, wl, ah, al, first, last):
                pe.matmul(dst, wh, ah, start=first, stop=False)
                pe.matmul(dst, wh, al, start=False, stop=False)
                return pe.matmul(dst, wl, ah, start=False, stop=last)

            def wait_unit(unit, shared):
                count = unit + 3
                pe.wait_ge(lo_done, count)
                if shared:
                    pe.wait_ge(lo_rest, count)

            def wblock(slot, at, m=P):
                return w_hi[slot][:, at:at + m], w_lo[slot][:, at:at + m]

            def keep_clock(b):
                for _ in range(3):
                    pe.matmul(bank[:, b, 0:TX], ident, const[:, C_COSB:C_COSB + TX], start=True, stop=True)

            def norm(r, w):
                if r % 3 == 2:
                    pe.wait_ge(mstat_used, 2 * (r // 3 + 1))
                keep_clock(BCAST)
                pe.wait_ge(sq_added, 8 * (r + 1) + 2)
                for j in range(w // P):
                    ins = pe.matmul(bank[:, STAT, j:j + 1], sq_sum[:, j * P:(j + 1) * P], col(COL_MODEL),
                                    start=True, stop=True)
                ins.then_inc(stat_ready, 1)
                keep_clock(BCAST)
                pe.wait_ge(diag_ready, r + 1)
                pe.matmul(bank[:, BCAST, 0:w], ones, diag[0][:, 0:w], start=True, stop=True).then_inc(bcast_ready, 1)
                keep_clock(STAT)

            def down(ub, vb, n, a_hi, a_lo, w, wait, shared):
                with pe.Fori(0, 2) as i:
                    for s in range(2):
                        wait_unit(ub + 2 * i + s, shared)
                        for d in range(2):
                            pe.wait_ge(x_done, vb + 4 * i + 2 * s + d + 1)
                            for k in range(n):
                                if s == 0 and d == 0:
                                    wait(k)
                                wh, wl = wblock(s, (d * n + k) * P)
                                ins = split_product(bank[:, 4 + d, 0:w], wh, wl, a_hi[:, k, 0:w], a_lo[:, k, 0:w],
                                                    k == 0, k == n - 1)
                            ins.then_inc(units_done if d else y_even, 1)

            def ffn(f, r):
                w, base, layer = width(f), ffn_base(f), f // 2
                start = 0
                for g, n in enumerate(GROUPS):
                    ub = base + UP_OFF[g]
                    with pe.Fori(0, n // 2) as i:
                        for s in range(2):
                            wait_unit(ub + 2 * i + s, f == 2 * DEPTH - 1)
                            pe.wait_ge(gu_used, FT * f + start + 2 * i + s + 1)
                            for k in range(KT):
                                if g == 0 and s == 0:
                                    pe.wait_ge(n_ready, 8 * r + k + 1)
                                for m in range(2):
                                    wh, wl = wblock(s, (m * KT + k) * P)
                                    ins = split_product(bank[:, 2 * s + m, 0:w], wh, wl, n_hi[:, k, 0:w], n_lo[:, k, 0:w],
                                                        k == 0, k == KT - 1)
                            ins.then_inc(units_done, 1)
                    start += n

                    def hidden_ready(k, n=n, start=start):
                        if k == 0:
                            pe.wait_ge(h_lo_done, FT * f + start - 2)
                        elif k >= n - 2:
                            pe.wait_ge(h_lo_done, FT * f + start - (n - 1 - k))

                    down(base + DOWN_OFF[g], visit_base(layer, 2 * (f % 2)) + g * KT, n, h_hi, h_lo, w, hidden_ready, f == 2 * DEPTH - 1)

            def project(layer, r):
                wq = T if layer < DEPTH - 1 else TX
                base = layer * LAYER_UNITS + MIX0
                rots = [0]
                n_sq = 0

                def rotate(lhs, rhs):
                    m = N_ROT * layer + rots[0]
                    if m >= 2:
                        pe.wait_ge(rot_used, m - 1)
                    pe.matmul(bank[0:lhs.shape[1], 4 + rots[0] % 2, 0:TX], lhs, rhs, start=True, stop=True).then_inc(rot_ready, 1)
                    rots[0] += 1

                def head_stats(k, c, w, sel):
                    pe.wait_ge(msq_ready, 8 * layer + k + 1)
                    for j in range(w // P):
                        dst = bank[:, STAT, 4 * c + j:4 * c + j + 5:4]
                        ins = pe.matmul(dst, squares[k % 2][:, j * P:(j + 1) * P], sel, start=True, stop=True)
                    ins.then_inc(msq_used, 1)

                def after(j):
                    kind, t = PROJ[j]
                    if kind == "bq":
                        head_stats(t, ST_Q + 2 * t, wq, col(COL_HEAD, 2))
                        pe.wait_ge(proj_used, N_PROJ * layer + j + 1)
                        rotate(const[:, C_ROTB:C_ROTB + P], bq[:, t, 0:TX])
                    elif kind == "bk":
                        head_stats(4, ST_K, T, col(COL_HEAD, 2))
                        pe.wait_ge(proj_used, N_PROJ * layer + j + 1)
                        rotate(const[:, C_ROTB:C_ROTB + P], bk[:, 0, 0:TX])
                    elif kind == "ckv":
                        pe.wait_ge(msq_ready, 8 * layer + 6)
                        for i in range(4):
                            ins = pe.matmul(bank[:, STAT, 4 * ST_CKV + i:4 * ST_CKV + i + 1], squares[1][:, i * P:(i + 1) * P],
                                            col(COL_CKV), start=True, stop=True)
                        ins.then_inc(msq_used, 1)
                    elif kind == "cq" and t == 1:
                        pe.wait_ge(msq_ready, 8 * layer + 8)
                        pe.wait_ge(mstat_used, 2 * layer + 1)
                        for i in range(wq // P):
                            for c in range(2):
                                ins = pe.matmul(bank[:, STAT, 4 * ST_CQ + i:4 * ST_CQ + i + 1],
                                                squares[c][:, i * P:(i + 1) * P], col(COL_CQ), start=c == 0, stop=c == 1)
                        ins.then_inc(msq_used, 2)
                    elif kind == "kr":
                        pe.wait_ge(proj_used, N_PROJ * layer + j + 1)
                        rotate(const[64:96, C_ROTM:C_ROTM + 96], mk[64:96, 0, 0:TX])
                    elif kind == "mq":
                        pe.wait_ge(proj_used, N_PROJ * layer + j + 1)
                        rotate(const[64:96, C_ROTM:C_ROTM + 96], mq[64:96, t, 0:TX])

                def keys_norm():
                    pe.wait_ge(mdiag_ready, 2 * layer + 1)
                    pe.matmul(bank[:, BCAST, :], const[:, C_SEL0:C_SEL0 + P], diag[0], start=True, stop=False)
                    pe.matmul(bank[:, BCAST, :], const[:, C_SEL1:C_SEL1 + P], diag[1], start=False, stop=True).then_inc(mbc_ready, 1)

                def latent_norm():
                    pe.wait_ge(mdiag_ready, 2 * layer + 2)
                    pe.matmul(bank[:, BCAST, :], ones, diag[0], start=True, stop=True).then_inc(mbc_ready, 1)

                for j, (kind, t) in enumerate(PROJ):
                    u = PROJ_UNIT[j]
                    s = u % 2
                    if j == 0 or PROJ_UNIT[j - 1] != u:
                        pe.wait_ge(lo_done, base + u + 3)
                    if j >= 4:
                        pe.wait_ge(proj_used, N_PROJ * layer + j - 3)
                    dst = bank[:, j % 4, :]
                    w = wq if kind in ("bq", "cq", "mq", "aq") else T
                    if j == 0:
                        for k in range(KT):
                            pe.wait_ge(n_ready, 8 * r + k + 1)
                            for m in range(2):
                                wh, wl = wblock(s, (KT * m + k) * P)
                                ins = split_product(bank[:, m, 0:w], wh, wl, n_hi[:, k, 0:w], n_lo[:, k, 0:w], k == 0, k == KT - 1)
                                if m == 0 and k == KT - 1:
                                    ins.then_inc(proj_mid, 1)
                        first_pair = ins
                        continue
                    if j == 1:
                        ins = first_pair
                    elif kind in ("bq", "bk", "ckv", "cq", "ak", "aq"):
                        second = proj_last(j)
                        for k in range(KT):
                            wh, wl = wblock(s, ((KT if second else 0) + k) * P)
                            ins = split_product(dst[:, 0:w], wh, wl, n_hi[:, k, 0:w], n_lo[:, k, 0:w], k == 0, k == KT - 1)
                    elif kind in ("vb", "va"):
                        cols, per = (P, 4) if kind == "vb" else (2 * P, 2)
                        for i in range(per):
                            tok = slice((per * t + i) * P, (per * t + i + 1) * P)
                            for k in range(KT):
                                wh, wl = wblock(s, k * cols, cols)
                                ins = split_product(dst[:, i * cols:(i + 1) * cols], n_hi[:, k, tok], n_lo[:, k, tok], wh, wl,
                                                    k == 0, k == KT - 1)
                    elif kind == "kr":
                        for k in range(KT):
                            wh, wl = wblock(s, 8 * P + k * MW, MW)
                            ins = split_product(dst[0:MW, :], wh, wl, n_hi[:, k, :], n_lo[:, k, :], k == 0, k == KT - 1)
                    elif kind == "mq":
                        if t == 0:
                            pe.wait_ge(lat_lo, 3 * layer + 2)
                        for k in range(2):
                            wh, wl = wblock(s, (k * 4 + t) * MW, MW)
                            ins = split_product(dst[0:MW, 0:w], wh, wl, h_hi[:, k, 0:w], h_lo[:, k, 0:w], k == 0, k == 1)
                    elif kind == "mk":
                        if t == 0:
                            pe.wait_ge(lat_lo, 3 * layer + 3)
                        wh, wl = wblock(s, t * P, HD)
                        ins = split_product(dst[0:HD, :], wh, wl, h_hi[:, 2, :], h_lo[:, 2, :], True, True)
                    elif kind == "vm":
                        for i in range(2):
                            tok = slice((2 * t + i) * P, (2 * t + i + 1) * P)
                            wh, wl = (x_[:, 0:512].rearrange("p (h c) -> p h c", h=4)[:, :, 64:128] for x_ in (w_hi[s], w_lo[s]))
                            ins = split_product(dst[:, i * 256:(i + 1) * 256].rearrange("p (h c) -> p h c", h=4),
                                                h_hi[:, 2, tok], h_lo[:, 2, tok], wh, wl, True, True)
                    ins.then_inc(units_done if proj_last(j) else proj_mid, 1)
                    after(j - 1)
                    if j == 8:
                        keys_norm()
                    if j == 9:
                        latent_norm()
                after(N_PROJ - 1)

            def attention(layer):
                todo = blocks(layer)
                b0 = block_base(layer)

                def scores(n):
                    kind, t, half, part, tile, _ = todo[n]
                    keys = slice(0, T) if part == 0 else slice(TX, T)
                    if n >= 2:
                        pe.wait_ge(exp_done, b0 + n - 1)
                    for q in range(2):
                        tok = slice((2 * part + q) * P, (2 * part + q + 1) * P)
                        if kind == "a":
                            lhs, rhs = aq[:, t, tok], (ak, ak_odd)[half][:, t, keys]
                        elif kind == "b":
                            lhs, rhs = bq[:, t, tok], bk[:, half, keys]
                        else:
                            lhs, rhs = mq[0:MW, 2 * t + half, tok], mk[0:MW, 2 * t + half, keys]
                        ins = pe.matmul(bank[:, 2 * (n % 2) + q, 0:keys.stop - keys.start], lhs, rhs, start=True, stop=True)
                    ins.then_inc(s_ready, 1)

                def transposes(n):
                    part = todo[n][3]
                    pe.wait_ge(p_ready, b0 + n + 1)
                    if n:
                        pe.wait_ge(pt_a, b0 + n)
                        if x_blocks(layer, n):
                            pe.wait_ge(pt_b, sum(x_blocks(i, N_BLOCKS[i]) for i in range(layer)) + x_blocks(layer, n))
                    for k in range(4 if part == 0 else 2):
                        for q in range(2):
                            dst = bank[:, 4 + k // 2, (k % 2) * TX + q * P:(k % 2) * TX + (q + 1) * P]
                            ins = pe.transpose(dst, probs[:, n % 2, q, k * P:(k + 1) * P], ident)
                    ins.then_inc(pt_ready, 1)

                def weigh(n):
                    kind, t, half, part, tile, last = todo[n]
                    pe.wait_ge(pt_a, b0 + n + 1)
                    if part == 0:
                        pe.wait_ge(pt_b, sum(x_blocks(i, N_BLOCKS[i]) for i in range(layer)) + x_blocks(layer, n + 1))
                    if half == 0 and part == 0 and 8 * layer + tile >= 2:
                        pe.wait_ge(o_lo, 8 * layer + tile - 1)
                    vcol = {"a": (2 * t + half) * HD, "b": 256 + half * HD, "m": 384 + (2 * t + half) * HD}[kind]
                    nk = 4 if part == 0 else 2
                    for k in range(nk):
                        keytile = k if part == 0 else 2 + k
                        ins = pe.matmul(bank[64 * half:64 * half + 64, 6 + tile % 2, part * TX:(part + 1) * TX],
                                        val[:, keytile, vcol:vcol + HD],
                                        tmp[:, 2 * (n % 2) + k // 2, (k % 2) * TX:(k % 2 + 1) * TX],
                                        start=k == 0, stop=k == nk - 1)
                    if last:
                        ins.then_inc(o_ready, 1)

                pe.wait_ge(proj_used, N_PROJ * (layer + 1))
                pe.wait_ge(rot_used, N_ROT * (layer + 1))
                pe.wait_ge(kv_ready, 3 * (layer + 1))
                scores(0)
                scores(1)
                for n in range(len(todo)):
                    if n + 2 < len(todo):
                        scores(n + 2)
                    transposes(n)
                    if n:
                        weigh(n - 1)
                weigh(len(todo) - 1)

            def merge(layer):
                w = T if layer < DEPTH - 1 else TX
                base = layer * LAYER_UNITS + MERGE0
                m0 = layer * KT
                pe.wait_ge(o_lo, 8 * (layer + 1))
                with pe.Fori(0, KT) as i:
                    d = m0 + i

                    def gate(slot, at, b):
                        for k in range(KT):
                            wh, wl = wblock(slot, (at + k) * P)
                            ins = split_product(bank[:, b, 0:w], wh, wl, n_hi[:, k, 0:w], n_lo[:, k, 0:w], k == 0, k == KT - 1)
                        return ins

                    def branch(at, first, n, b):
                        pe.wait_ge(mg_used, 3 * d + b + 1)
                        for k in range(n):
                            wh, wl = wblock(1, (at + k) * P)
                            ins = split_product(bank[:, (3, 6, 7)[b], 0:w], wh, wl, h_hi[:, first + k, 0:w],
                                                h_lo[:, first + k, 0:w], k == 0, k == n - 1)
                        return ins

                    wait_unit(base + 2 * i, layer == DEPTH - 1)
                    pe.wait_ge(mg_tanh, 3 * d + 1)
                    gate(0, 0, 0).then_inc(mg_ready, 1)
                    pe.wait_ge(mg_tanh, 3 * d + 2)
                    gate(0, KT, 1).then_inc(units_done, 1)
                    wait_unit(base + 2 * i + 1, layer == DEPTH - 1)
                    pe.wait_ge(mg_tanh, 3 * d + 3)
                    gate(1, 0, 2).then_inc(mg_ready, 1)
                    branch(KT, 0, 2, 0).then_inc(mg_ready, 1)
                    branch(KT + 2, 2, 4, 1).then_inc(mg_ready, 1)
                    branch(KT + 6, 6, 2, 2).then_inc(units_done, 1)

                def merged_ready(k):
                    if k == 0 or k >= KT - 2:
                        pe.wait_ge(yl_done, m0 + (k + 2 if k else KT - 1))

                down(layer * LAYER_UNITS + OUT0, visit_base(layer, 1), KT, y_hi, y_lo, w, merged_ready, layer == DEPTH - 1)

            pe.sem_inc(units_done, 2)
            pe.wait_ge(s_const, 32)
            norm(0, T)
            for layer in range(DEPTH):
                r = 3 * layer
                w = T if layer < DEPTH - 1 else TX
                if layer:
                    norm(r, T)
                ffn(2 * layer, r)
                norm(r + 1, T)
                project(layer, r + 1)
                attention(layer)
                merge(layer)
                norm(r + 2, w)
                ffn(2 * layer + 1, r + 2)
            norm(3 * DEPTH, TX)

        @block.vector
        def _(dve):
            steps = [0]

            def then(ins):
                steps[0] += 1
                ins.then_inc(v_step, 1)
                dve.wait_ge(v_step, steps[0])

            def rsqrt(dst, src, shape):
                v, a, b = (shape(t) for t in (rs_v, rs_a, rs_b))
                then(dve.tensor_scalar(v, src, EPS, None, ALU.add))
                then(dve.tensor_scalar(b.bitcast(I32), v.bitcast(I32), 1, None, ALU.logical_shift_right))
                then(dve.tensor_scalar(dst.bitcast(I32), b.bitcast(I32), -1.0, RSQRT_MAGIC, ALU.mult, ALU.add))
                for _ in range(3):
                    then(dve.tensor_tensor(a, dst, dst, ALU.mult))
                    then(dve.scalar_tensor_tensor(b, a, -0.5, v, ALU.mult, ALU.mult))
                    then(dve.scalar_tensor_tensor(dst, b, 1.5, dst, ALU.add, ALU.mult))

            def silu_conditions(f):
                dve.wait_ge(cond_tanh, f + 1)
                then(dve.scalar_tensor_tensor(ada_junk[:, :, :], ada_junk[:, :, :], 1.0, silu_b[:, :, :], ALU.add, ALU.mult))
                then(dve.tensor_scalar(silu_b[:, :, :], ada_junk[:, :, :], 0.5, None, ALU.mult))

            def ada_half(piece, half, helped=False):
                dve.wait_ge(ada_in[half], 16 * (piece + 1))
                for t in range(2):
                    for v in range(2):
                        n = 4 * half + 2 * t + v
                        if helped and t == v == 1:
                            dve.wait_ge(ada_step, 8 * piece + n + 2)
                            dve.wait_ge(help_product, 2 * piece + half + 1)
                            dve.sem_inc(ada_step, 1)
                            continue
                        dve.wait_ge(ada_step, 8 * piece + n + 1)
                        dve.scalar_tensor_tensor(ada_junk[:, v, :], ada_raw[half][:, t, :], 1.0, silu_b[:, v, :],
                                                 ALU.mult, ALU.mult,
                                                 accum_out=mods[:, v, bass.ds(piece * 4 + 2 * half + t, 1)]).then_inc(ada_step, 1)
                dve.wait_ge(ada_step, 8 * piece + 4 * half + 6)
                dve.sem_inc(ada_used, 1)

            def ada_out(piece):
                for v in range(2):
                    at = mods[:, v, bass.ds(piece * 4, 4)]
                    ins = dve.tensor_tensor(at, at, gains[:, bass.ds(piece * 4 + G_BADA, 4)], ALU.add)
                ins.then_inc(ada_done, 1)

            def rest_lo(base, i, s):
                dve.wait_ge(hi_rest, base + 2 * i + s + 2 - SHARED0 + 1)
                dve.tensor_tensor(w_lo[s][:, OWN:], w_raw[s][:, OWN:], w_hi[s][:, OWN:].bitcast(F32),
                                  ALU.subtract).then_inc(lo_rest, 1)

            def add_square(q, w, parity):
                dve.wait_ge(sq_done, q + 1)
                dve.wait_ge(sq_added, q + 2)
                dve.tensor_tensor(sq_sum[:, 0:w], sq_sum[:, 0:w], squares[parity][:, 0:w], ALU.add).then_inc(sq_added, 1)

            def mod_col(layer, m):
                return layer * N_MOD * KT + m * KT

            def norm(r, layer, m, gain, w):
                nj = w // P
                if layer is not None:
                    at = mod_col(layer, m + 1)
                    dve.wait_ge(ada_done, layer * LP + 2 * (m + 2))
                    for v in range(2):
                        ins = dve.scalar_tensor_tensor(coef_a[:, v, :], mods[:, v, at:at + KT], 1.0, gains[:, gain:gain + KT],
                                                       ALU.add, ALU.mult)
                    then(ins)
                dve.wait_ge(stat_ready, r + 1)
                rsqrt(rstd[:, 0:nj], bank[:, STAT, 0:nj], lambda t: t[:, 0:nj])
                for j in range(nj):
                    ins = dve.tensor_scalar(diag[0][:, j * P:(j + 1) * P], ident, rstd[:, j:j + 1], None, ALU.mult)
                ins.then_inc(diag_ready, 1)
                dve.wait_ge(bcast_ready, r + 1)

                def low(dt):
                    dve.wait_ge(n_hi_done, 8 * r + dt + 1)
                    dve.tensor_tensor(n_lo[:, dt, 0:w], tmp[:, 2 + dt % 2, 0:w], n_hi[:, dt, 0:w].bitcast(F32),
                                      ALU.subtract).then_inc(n_ready, 1)

                for dt in range(KT):
                    if layer is None:
                        if dt >= 2:
                            dve.wait_ge(fin_o, dt - 1)
                        dve.tensor_tensor(tmp[:, dt % 2, 0:w], x[:, dt, 0:w], bank[:, BCAST, 0:w], ALU.mult).then_inc(fin_t, 1)
                        continue
                    dve.tensor_tensor(tmp[:, dt % 2, 0:w], x[:, dt, 0:w], bank[:, BCAST, 0:w], ALU.mult).then_inc(scaled, 1)
                    if dt:
                        low(dt - 1)
                if layer is not None:
                    low(KT - 1)

            def gate_coef(layer, m, factor):
                at = mod_col(layer, m)
                dve.wait_ge(ada_done, layer * LP + 2 * (m + 1))
                then(dve.tensor_scalar(coef_g[:, :, :], mods[:, :, at:at + KT], factor, None, ALU.mult))

            def clear_squares():
                then(dve.memset(sq_sum[:, :], 0.0))

            def down(ub, vb, yb, w, q0, extra=None, shared=False, ends=False):
                def step(i, more):
                    for s in range(2):
                        if extra is not None:
                            ada_half(extra + i, s)
                        for d in range(2):
                            dt = 4 * i + 2 * s + d
                            if d == 0:
                                dve.wait_ge(y_even, yb + 2 * i + s + 1)
                            else:
                                dve.wait_ge(units_done, ub + 2 * i + s + 3)
                            for v in range(w // TX):
                                tile = tile_of(x, dt, TX, v * TX)
                                ins = dve.scalar_tensor_tensor(tile, bank[:, 4 + d, v * TX:(v + 1) * TX],
                                                               coef_g[:, v, bass.ds(dt, 1)], tile, ALU.mult, ALU.add)
                            ins.then_inc(x_done, 1)
                        if q0 is not None:
                            for d in range(2):
                                add_square(q0 + 4 * i + 2 * s + d, w, d)
                        if shared and more:
                            rest_lo(ub, i, s)
                    if extra is not None:
                        ada_out(extra + i)

                if ends:
                    step(0, True)
                    step(1, False)
                else:
                    with dve.Fori(0, 2) as i:
                        step(i, True)

            def ffn(f, q0):
                w, base, layer = width(f), ffn_base(f), f // 2
                start = 0
                for g, n in enumerate(GROUPS):
                    if f == 1 and g == 1:
                        silu_conditions(f)
                    ub = base + UP_OFF[g]
                    carries = (f, g) in ADA_UP
                    with dve.Fori(0, n // 2) as i:
                        for s in range(2):
                            tile = FT * f + start + 2 * i + s
                            if carries:
                                ada_half(ADA_UP[f, g] + i, s)
                            dve.wait_ge(tanh_done, tile + 1)
                            dve.scalar_tensor_tensor(tmp[:, 2 + s, 0:w], tmp[:, s, 0:w], 1.0, bank[:, 2 * s, 0:w],
                                                     ALU.add, ALU.mult).then_inc(silu_done, 1)
                            dve.wait_ge(silu_done, tile + 1)
                            dve.tensor_tensor(tmp[:, 4 + s, 0:w], tmp[:, 2 + s, 0:w], bank[:, 2 * s + 1, 0:w],
                                              ALU.mult).then_inc(gu_used, 1)
                            if f == 2 * DEPTH - 1:
                                rest_lo(ub, i, s)
                            dve.wait_ge(h_hi_done, tile + 1)
                            dve.tensor_tensor(tile_of(h_lo, 2 * i + s, w), tmp[:, 4 + s, 0:w],
                                              tile_of(h_hi, 2 * i + s, w).bitcast(F32),
                                              ALU.subtract).then_inc(h_lo_done, 1)
                        if carries:
                            ada_out(ADA_UP[f, g] + i)
                    start += n
                    if g == 0:
                        gate_coef(layer, 2 + 6 * (f % 2), 0.25)
                    if g == 2:
                        clear_squares()
                    yb = (f // 2) * 28 + (f % 2) * 16 + 4 * g
                    down(base + DOWN_OFF[g], visit_base(layer, 2 * (f % 2)) + g * KT, yb, w, q0 if g == 2 else None,
                         ADA_DOWN.get((f, g)), f == 2 * DEPTH - 1, f == 2 * DEPTH - 1 and g == 2)

            def project(layer):
                wq = T if layer < DEPTH - 1 else TX
                njq = wq // P
                cosb, sinb = const[:, C_COSB:C_COSB + TX], const[:, C_SINB:C_SINB + TX]
                rots = [0]

                def rope(dst, rows, cos, sin):
                    m = N_ROT * layer + rots[0]
                    b = 4 + rots[0] % 2
                    dve.wait_ge(rot_ready, m + 1)
                    if m:
                        dve.wait_ge(rot_used, m)
                    then(dve.tensor_tensor(tmp[rows, 3, 0:TX], bank[rows, b, 0:TX], sin[rows, :], ALU.mult))
                    then(dve.tensor_tensor(dst, dst, cos[rows, :], ALU.mult))
                    dve.tensor_tensor(dst, dst, tmp[rows, 3, 0:TX], ALU.add).then_inc(rot_used, 1)
                    rots[0] += 1

                def diagonal(which, c):
                    for j in range(4):
                        ins = dve.tensor_scalar(diag[which][:, j * P:(j + 1) * P], ident, rstd[:, 4 * c + j:4 * c + j + 1],
                                                None, ALU.mult)
                    return ins

                def latent_lo(t, i, w):
                    dve.wait_ge(lat_hi, 3 * layer + i + 1)
                    src = tmp[:, (1, 2, 0)[i], 0:w]
                    dve.tensor_tensor(h_lo[:, t, 0:w], src, h_hi[:, t, 0:w].bitcast(F32), ALU.subtract).then_inc(lat_lo, 1)

                dve.memset(bk[0:64, 1, :], 0.0)
                dve.memset(ak[64:128, :, :], 0.0)
                dve.memset(ak_odd[0:64, :, :], 0.0).then_inc(zeroed, 1)
                full = slice(0, P)
                for t in range(4):
                    rope(bq[:, t, 0:TX], full, cosb, sinb)
                rope(bk[:, 0, 0:TX], full, cosb, sinb)
                dve.wait_ge(msq_used, 8 * layer + 6)
                then(dve.tensor_scalar(rs_v[:, 0:12], bank[:, STAT, 0:12], EPS, None, ALU.add))
                dve.sem_inc(mstat_used, 1)
                rsqrt_from_v(rstd[:, 0:12], lambda t: t[:, 0:12])
                diagonal(0, ST_K)
                diagonal(1, ST_K + 1).then_inc(mdiag_ready, 1)
                latent_lo(0, 0, wq)
                latent_lo(1, 1, wq)
                dve.wait_ge(mbc_ready, 2 * layer + 1)
                dve.wait_ge(rot_used, N_ROT * layer + 5)
                dve.tensor_tensor(bk[0:64, 0, :], bk[0:64, 0, :], bank[0:64, BCAST, :], ALU.mult)
                then(dve.tensor_tensor(bk[64:128, 1, :], bk[64:128, 0, :], bank[64:128, BCAST, :], ALU.mult))
                then(dve.memset(bk[64:128, 0, :], 0.0))
                diagonal(0, ST_CKV).then_inc(mdiag_ready, 1)
                dve.wait_ge(mbc_ready, 2 * layer + 2)
                dve.wait_ge(proj_used, N_PROJ * layer + 6)
                dve.tensor_tensor(tmp[:, 0, :], tmp[:, 0, :], bank[:, BCAST, :], ALU.mult).then_inc(lat_f32, 1)
                latent_lo(2, 2, T)
                dve.wait_ge(msq_used, 8 * layer + 8)
                c0 = 4 * ST_CQ

                def shape(t):
                    return t[:, c0:48].rearrange("p (c j) -> p c j", j=4)[:, :, 0:njq]

                then(dve.tensor_scalar(shape(rs_v), bank[:, STAT, c0:48].rearrange("p (c j) -> p c j", j=4)[:, :, 0:njq],
                                       EPS, None, ALU.add))
                dve.sem_inc(mstat_used, 1)
                rsqrt_from_v(shape(rstd), shape)
                qs = qscale[:, :].rearrange("p (c j) -> p c j", j=4)[:, :, 0:njq]
                dve.tensor_scalar(qs[:, 0:1], shape(rstd)[:, 0:1], MLA_SCALE, None, ALU.mult)
                then(dve.tensor_scalar(qs[:, 1:9], shape(rstd)[:, 1:9], HD ** -0.5, None, ALU.mult))
                cosm, sinm = const[:, C_COSM:C_COSM + TX], const[:, C_SINM:C_SINM + TX]
                rows = slice(64, 96)
                rope(mk[rows, 0, 0:TX], rows, cosm, sinm)
                for t in range(4):
                    rope(mq[rows, t, 0:TX], rows, cosm, sinm)
                if layer == DEPTH - 1:
                    for s in range(2):
                        rest_lo(layer * LAYER_UNITS + MERGE0 - 2, 0, s)

            def rsqrt_from_v(dst, shape):
                v, a, b = (shape(t) for t in (rs_v, rs_a, rs_b))
                then(dve.tensor_scalar(b.bitcast(I32), v.bitcast(I32), 1, None, ALU.logical_shift_right))
                then(dve.tensor_scalar(dst.bitcast(I32), b.bitcast(I32), -1.0, RSQRT_MAGIC, ALU.mult, ALU.add))
                for _ in range(3):
                    then(dve.tensor_tensor(a, dst, dst, ALU.mult))
                    then(dve.scalar_tensor_tensor(b, a, -0.5, v, ALU.mult, ALU.mult))
                    then(dve.scalar_tensor_tensor(dst, b, 1.5, dst, ALU.add, ALU.mult))

            def attention(layer):
                todo = blocks(layer)
                b0 = block_base(layer)
                mask = const[:, C_MASK:C_MASK + TX]

                def front(n):
                    kind, t, half, part, tile, _ = todo[n]
                    keys = T if part == 0 else TX
                    p = n % 2
                    banks = bank[:, 2 * p:2 * p + 2, :]
                    if kind == "a" and part == 0:
                        h = 2 * t + half
                        bias = tmp[:, 4 + h % 2, :].rearrange("p (q k) -> p q k", q=2)
                        dve.wait_ge(bias_in[h % 2], 64 * (2 * layer + h // 2 + 1))
                        for q in range(2):
                            ins = dve.scalar_tensor_tensor(bias[:, q, :], bias[:, q, :], 1.0 / NA_SCALE, mask, ALU.mult, ALU.add)
                        then(ins)
                        dve.wait_ge(s_ready, b0 + n + 1)
                        dve.tensor_tensor(banks[:, :, 0:TX], banks[:, :, 0:TX], bias, ALU.add).then_inc(bias_used, 1)
                        dve.wait_ge(bias_used, 4 * layer + h + 1)
                    dve.wait_ge(s_ready, b0 + n + 1)
                    then(dve.tensor_reduce(mx[:, p, :], banks[:, :, 0:keys], AX.X, ALU.max))
                    if kind == "a":
                        dve.tensor_scalar(nbias[:, p, :], mx[:, p, :], -NA_SCALE, None, ALU.mult).then_inc(nb_ready, 1)
                    else:
                        c = (0 if kind == "m" else 4 * (1 + 2 * t + half)) + 2 * part
                        dve.scalar_tensor_tensor(nbias[:, p, :], mx[:, p, :], -1.0, qscale[:, c:c + 2],
                                                 ALU.mult, ALU.mult).then_inc(nb_ready, 1)

                def back(n):
                    part, p = todo[n][3], n % 2
                    keys = T if part == 0 else TX
                    dve.wait_ge(exp_done, b0 + n + 1)
                    then(dve.reciprocal(rinv[:, p, :], rsum[:, p, :]))
                    for q in range(2):
                        ins = dve.tensor_scalar(probs[:, p, q, 0:keys], probs[:, p, q, 0:keys], rinv[:, p, q:q + 1], None, ALU.mult)
                    ins.then_inc(p_ready, 1)

                def out_lo(n):
                    tile = todo[n][4]
                    w = T if layer < DEPTH - 1 else TX
                    dve.wait_ge(o_hi, 8 * layer + tile + 1)
                    dve.tensor_tensor(h_lo[:, tile, 0:w], bank[:, 6 + tile % 2, 0:w], h_hi[:, tile, 0:w].bitcast(F32),
                                      ALU.subtract).then_inc(o_lo, 1)

                front(0)
                front(1)
                for n in range(len(todo)):
                    back(n)
                    if n + 2 < len(todo):
                        front(n + 2)
                    if todo[n][3] == 0:
                        dve.wait_ge(pt_ready, b0 + n + 1)
                        dve.tensor_copy(tmp[:, 2 * (n % 2) + 1, :], bank[:, 5, :]).then_inc(pt_b, 1)
                    if n >= 2 and todo[n - 2][5]:
                        out_lo(n - 2)
                out_lo(len(todo) - 1)

            def merge(layer, q0):
                w = T if layer < DEPTH - 1 else TX
                base = layer * LAYER_UNITS + MERGE0
                m0 = layer * KT
                gate_coef(layer, 5, 0.5)
                with dve.Fori(0, KT) as i:
                    d = m0 + i
                    if layer == DEPTH - 1:
                        rest_lo(base, i, 0)
                    for b in range(3):
                        if b < 2:
                            dve.wait_ge(mg_ready, 4 * d + 3 + b)
                        else:
                            dve.wait_ge(units_done, base + 2 * i + 4)
                        dve.wait_ge(mg_tanh, 3 * d + b + 4)
                        if b == 1:
                            dve.wait_ge(yl_done, d + 1)
                        dve.scalar_tensor_tensor(tmp[:, 3 + b, 0:w], tmp[:, b, 0:w], 1.0, bank[:, (3, 6, 7)[b], 0:w],
                                                 ALU.add, ALU.mult).then_inc(mg_used, 1)
                        if b == 1:
                            dve.wait_ge(mg_used, 3 * d + 5)
                            dve.tensor_tensor(tmp[:, 3, 0:w], tmp[:, 3, 0:w], tmp[:, 4, 0:w], ALU.add).then_inc(mg_add, 1)
                    dve.wait_ge(mg_used, 3 * d + 6)
                    dve.wait_ge(mg_add, d + 1)
                    dve.tensor_tensor(tmp[:, 4, 0:w], tmp[:, 3, 0:w], tmp[:, 5, 0:w], ALU.add).then_inc(mg_y, 1)
                    if layer == DEPTH - 1:
                        rest_lo(base, i, 1)
                    dve.wait_ge(yh_done, d + 1)
                    dve.tensor_tensor(tile_of(y_lo, i, w), tmp[:, 4, 0:w],
                                      tile_of(y_hi, i, w).bitcast(F32),
                                      ALU.subtract).then_inc(yl_done, 1)
                clear_squares()
                down(layer * LAYER_UNITS + OUT0, visit_base(layer, 1), layer * 28 + 12, w, q0, shared=layer == DEPTH - 1)

            dve.sem_inc(lo_rest, SHARED0 + 2)
            dve.sem_inc(ada_used, 2)
            dve.sem_inc(ada_step, 2)
            dve.sem_inc(sq_added, 2)
            dve.sem_inc(gu_used, 2)
            dve.sem_inc(x_done, 2)
            dve.sem_inc(mg_used, 3)
            dve.sem_inc(yl_done, 1)
            clear_squares()
            dve.wait_ge(s_const, 32)
            silu_conditions(0)
            dve.sem_inc(silu_ready, 1)
            for piece in range(EARLY_PIECES):
                if piece == 1:
                    for dt in range(KT):
                        add_square(dt, T, dt % 2)
                ada_half(piece, 0, True)
                ada_half(piece, 1, True)
                dve.wait_ge(help_sum, 2 * piece + 2)
                ada_out(piece)
            norm(0, 0, 0, G_FFN1, T)
            for layer in range(DEPTH):
                r, g0 = 3 * layer, layer * G_LAYER
                w = T if layer < DEPTH - 1 else TX
                if layer:
                    norm(r, layer, 0, g0 + G_FFN1, T)
                ffn(2 * layer, 8 + 24 * layer)
                norm(r + 1, layer, 3, g0 + G_MIX, T)
                project(layer)
                attention(layer)
                merge(layer, 8 + 24 * layer + 8)
                norm(r + 2, layer, 6, g0 + G_FFN2, w)
                ffn(2 * layer + 1, 8 + 24 * layer + 16)
            norm(3 * DEPTH, None, 0, 0, TX)


def _constants():
    import numpy as np
    c = np.zeros((P, C_WIDTH), np.float32)
    c[:, C_ID:C_ID + P] = np.eye(P)
    c[:, C_ONES:C_ONES + P] = 1.0
    c[:, C_SEL0:C_SEL0 + HD] = 1.0
    c[:, C_SEL1 + HD:C_SEL1 + P] = 1.0

    def rotation(width):
        r = np.zeros((width, width), np.float32)
        q = width // 4
        for half in range(2):
            for i in range(q):
                a, b = half * 2 * q + i, half * 2 * q + q + i
                r[b, a] = -1.0
                r[a, b] = 1.0
        return r

    for h in range(2):
        c[h * HD:(h + 1) * HD, C_ROTB + h * HD:C_ROTB + (h + 1) * HD] = rotation(HD)
    c[HD:MW, C_ROTM + HD:C_ROTM + MW] = rotation(ROPE_M)

    cols = np.arange(GRID_W)
    c0 = np.clip(cols - 8, 0, GRID_W - 16)
    inside = (cols[None, :] >= c0[:, None]) & (cols[None, :] < c0[:, None] + 16)
    mask = np.where(inside, np.float32(0.0), np.float32(-1e30 / NA_SCALE))
    c[:, C_MASK:C_MASK + TX] = np.tile(mask, (2, 4))

    def table(width):
        half = width // 2
        freqs = np.float32(10000.0) ** (-np.arange(0, half, 2, dtype=np.float32) / np.float32(half))
        t = np.arange(TX)
        row = (t // GRID_W).astype(np.float32)[:, None] * freqs
        colm = (t % GRID_W).astype(np.float32)[:, None] * freqs
        ang = np.concatenate([row, row, colm, colm], axis=-1).astype(np.float32).T
        return np.cos(ang), np.sin(ang)

    cosb, sinb = table(HD)
    c[:, C_COSB:C_COSB + TX] = np.tile(cosb, (2, 1))
    c[:, C_SINB:C_SINB + TX] = np.tile(sinb, (2, 1))
    cosm, sinm = table(ROPE_M)
    c[HD:MW, C_COSM:C_COSM + TX] = cosm
    c[HD:MW, C_SINM:C_SINM + TX] = sinm
    c[:, C_COL + COL_MODEL] = 1.0 / D_MODEL
    c[0:HD, C_COL + COL_HEAD] = 1.0 / HD
    c[HD:P, C_COL + COL_HEAD + 1] = 1.0 / HD
    c[:, C_COL + COL_CQ] = 1.0 / 256
    c[:, C_COL + COL_CKV] = 1.0 / 128
    c[:, C_COL + COL_ONE] = 1.0
    return c


def _lay_out(a):
    import numpy as np

    def fm(v):
        return v.reshape(v.shape[:-1] + (-1, P)).swapaxes(-1, -2)

    def blocks(w, m=P):
        k, n = w.shape[-2:]
        b = w.reshape(w.shape[:-2] + (k // P, P, n // m, m))
        return np.moveaxis(b, (-4, -3, -2, -1), (-2, -3, -4, -1))

    d = {}
    both = np.concatenate([a["x"][0], a["ctx"][0]], axis=0)
    d["x_t"] = np.ascontiguousarray(both.T.reshape(KT, P, T).transpose(1, 0, 2))
    gates = np.stack([a["ffn1_w_gate"], a["ffn2_w_gate"]], 1).reshape(2 * DEPTH, D_MODEL, D_FF)
    ups = np.stack([a["ffn1_w_up"], a["ffn2_w_up"]], 1).reshape(2 * DEPTH, D_MODEL, D_FF)
    up = np.stack([blocks(gates), blocks(ups)], 3)
    d["w_up"] = np.ascontiguousarray(up.reshape(2 * DEPTH, FT, P, UNIT))
    downs = np.stack([a["ffn1_w_down"], a["ffn2_w_down"]], 1).reshape(2 * DEPTH, D_FF, D_MODEL)
    db = blocks(downs)
    db = db.reshape(2 * DEPTH, KT // 2, 2, P, FT, P).transpose(0, 1, 3, 2, 4, 5)
    first = np.stack([db[..., 0:8, :], db[..., 8:16, :]], 1)
    d["w_down"] = np.ascontiguousarray(first.reshape(2 * DEPTH, 2, KT // 2, P, UNIT))
    d["w_down_last"] = np.ascontiguousarray(db[..., 16:22, :].reshape(2 * DEPTH, KT // 2, P, 12 * P))
    ada = a["w_ada"].transpose(0, 2, 1).reshape(PIECES, 2, 2, P, D_MODEL)
    d["w_ada"] = np.ascontiguousarray(ada.transpose(0, 1, 3, 2, 4))
    d["cond"] = np.ascontiguousarray(np.stack([a["c"][0], a["c_ctx"]]))

    w_in = a["w_in"]
    q_order = np.concatenate([np.arange(64) + 64 * h for t in range(4) for h in (t, 4 + t)])
    s = np.cumsum([0, 256, 256, 256, 512, 128, 128, 256, 128, 32, 3072])
    part = {n: w_in[:, :, s[i]:s[i + 1]] for i, n in enumerate(("aq", "ak", "av", "bq", "bk", "bv", "cq", "ckv", "kr", "gate"))}
    part["bq"] = part["bq"][:, :, q_order]

    def rows(w):
        return w.reshape(DEPTH, -1, P, w.shape[-1]).transpose(0, 2, 1, 3).reshape(DEPTH, P, -1)

    def pair(w):
        return blocks(w).transpose(0, 2, 1, 3, 4).reshape(DEPTH, P, -1)

    kr = np.concatenate([np.zeros((DEPTH, D_MODEL, HD), np.float32), part["kr"]], -1)
    mix = [pair(part["bq"][:, :, 0:256]), pair(part["bq"][:, :, 256:512]),
           pair(np.concatenate([part["bk"], part["ckv"]], -1)), pair(part["cq"]),
           rows(part["bv"]), rows(kr), rows(a["mla_w_uq"]), rows(a["mla_w_ukv"]),
           pair(part["ak"]), pair(part["aq"]), rows(part["av"])]
    d["w_mix"] = np.ascontiguousarray(np.concatenate(mix, -1))
    gate = blocks(part["gate"]).reshape(DEPTH, 3, KT, P, KT, P)
    wb = a["w_branch_b"][:, q_order, :]
    br = np.concatenate([blocks(a["w_branch_a"]), blocks(wb), blocks(a["w_branch_c"])], 3)
    u0 = np.stack([gate[:, 0], gate[:, 1]], 3)
    u1 = np.stack([gate[:, 2], br], 3)
    d["w_merge"] = np.ascontiguousarray(np.stack([u0, u1], 2).reshape(DEPTH, 2 * KT, P, UNIT))
    wo = blocks(a["w_out"]).reshape(DEPTH, KT // 2, 2, P, KT, P).transpose(0, 1, 3, 2, 4, 5)
    d["w_out"] = np.ascontiguousarray(wo.reshape(DEPTH, KT // 2, P, UNIT))
    d["rel_bias"] = np.tile(a["na_rel_bias"], GRID_W)

    cols = []
    for i in range(DEPTH):
        cols += [fm(a["ffn1_norm"][i]), fm(a["mix_norm"][i]), fm(a["ffn2_norm"][i]), fm(a["mla_q_norm"][i]),
                 fm(a["mla_kv_norm"][i]), np.tile(a["gqa_q_norm"][i], 2)[:, None], np.tile(a["gqa_k_norm"][i], 2)[:, None]]
    cols += [fm(a["final_norm"])]
    cols += [fm(a["b_ada"][i]) for i in range(DEPTH)]
    d["gains"] = np.ascontiguousarray(np.concatenate(cols, 1))
    d["const"] = _constants()
    return d


def kernel(**inputs):
    import numpy as np
    import concourse.bacc as bacc
    from concourse.bass_utils import run_bass_kernel_spmd

    arrays = _lay_out({k: np.asarray(v) for k, v in inputs.items()})
    nc = bacc.Bacc("TRN2", target_bir_lowering=False, num_devices=1)
    dram = {n: nc.dram_tensor(n, v.shape, mybir.dt.from_np(v.dtype), kind="ExternalInput").ap() for n, v in arrays.items()}
    out = nc.dram_tensor("out_t", (P, KT, TX), F32, kind="ExternalOutput").ap()
    build(nc, dram, out)
    r = run_bass_kernel_spmd(nc, [arrays], core_ids=[0])
    got = r.results[0]["out_t"]
    return np.ascontiguousarray(got.transpose(2, 1, 0).reshape(1, TX, D_MODEL))
```
